# Optimizing a Trainium2 kernel written in Bass

```python
import math
import jax, jax.numpy as jnp
from jax import lax
import numpy as np

D_MODEL = 1024
BATCH = 1
SEQ = 512
DEPTH = 1

N_MIXERS = 2
EPS = 1e-6
POOL_WINDOWS = (2, 4, 8, 16)
POOL_GROUPS = 4
POOL_GC = D_MODEL // POOL_GROUPS
MLSTM_HEADS = 8
MLSTM_DV = D_MODEL // MLSTM_HEADS
MLSTM_DQK = MLSTM_DV // 2
QK_W = MLSTM_HEADS * MLSTM_DQK
V_W = MLSTM_HEADS * MLSTM_DV
IN_W = 2 * QK_W + 2 * V_W + 2 * MLSTM_HEADS
CONV_K = 4
CHUNK = 64
N_GROUPS = 4
EXPERTS_PER_GROUP = 4
N_EXPERTS = N_GROUPS * EXPERTS_PER_GROUP
TOP_K = 2
D_FF_EXPERT = D_MODEL // 2
N_POOL = (DEPTH + N_MIXERS - 1) // N_MIXERS
N_MLSTM = DEPTH // N_MIXERS

kernel_name = "hybrid_pool_mlstm_hmoe"

def rmsnorm(x, g):
    xf = x.astype(jnp.float32)
    y = xf * lax.rsqrt(jnp.mean(xf * xf, axis=-1, keepdims=True) + EPS)
    return (y * g.astype(jnp.float32)).astype(x.dtype)

def pool_mixer(xn, w_pool, scale):
    B, S, D = xn.shape
    xf = xn.astype(jnp.float32)
    cs = jnp.pad(jnp.cumsum(xf, axis=1), ((0, 0), (1, 0), (0, 0)))
    t = jnp.arange(S, dtype=jnp.float32)
    outs = []
    for g, w in enumerate(POOL_WINDOWS):
        sl = slice(g * POOL_GC, (g + 1) * POOL_GC)
        c = cs[..., sl]
        upper = c[:, 1:]
        lower = jnp.pad(c[:, :S + 1 - w], ((0, 0), (w - 1, 0), (0, 0)))
        count = jnp.minimum(t + 1.0, float(w))
        outs.append((upper - lower) / count[None, :, None] - xf[..., sl])
    pooled = jnp.stack(outs, axis=2).astype(xn.dtype)
    y = jnp.einsum('bsgc,gcd->bsgd', pooled, w_pool).reshape(B, S, D)
    return y * scale

def causal_conv(x, w, b):
    C = x.shape[-1]
    y = lax.conv_general_dilated(x, w[:, None, :].astype(x.dtype), window_strides=(1,),
                                 padding=[(CONV_K - 1, 0)],
                                 dimension_numbers=('NWC', 'WIO', 'NWC'),
                                 feature_group_count=C)
    return y + b.astype(x.dtype)

def mlstm_chunkwise(q, k, v, li, lf):
    B, S, H, dk = q.shape
    dv = v.shape[-1]
    L = CHUNK
    NC = S // L

    def chunks4(a):
        return a.reshape(B, NC, L, H, a.shape[-1]).transpose(1, 0, 3, 2, 4)

    def chunks3(a):
        return a.reshape(B, NC, L, H).transpose(1, 0, 3, 2)

    mask = jnp.tril(jnp.ones((L, L), dtype=bool))

    def step(carry, xs):
        C, n, m = carry
        qc, kc, vc, lic, lfc = xs
        b = jnp.cumsum(lfc, axis=-1)
        dmat = jnp.where(mask, b[..., :, None] - b[..., None, :] + lic[..., None, :], -jnp.inf)
        inter = b + m[..., None]
        m_t = jnp.maximum(inter, jnp.max(dmat, axis=-1))
        scores = jnp.einsum('bhtd,bhsd->bhts', qc, kc) * jnp.exp(dmat - m_t[..., None])
        s_inter = jnp.exp(inter - m_t)
        num = (jnp.einsum('bhts,bhsv->bhtv', scores, vc)
               + s_inter[..., None] * jnp.einsum('bhvd,bhtd->bhtv', C, qc))
        den = jnp.sum(scores, axis=-1) + s_inter * jnp.einsum('bhd,bhtd->bht', n, qc)
        h = num / jnp.maximum(jnp.abs(den), jnp.exp(-m_t))[..., None]
        bL = b[..., -1]
        g = bL[..., None] - b + lic
        m_new = jnp.maximum(bL + m, jnp.max(g, axis=-1))
        w_s = jnp.exp(g - m_new[..., None])
        decay = jnp.exp(bL + m - m_new)
        C_new = decay[..., None, None] * C + jnp.einsum('bhs,bhsv,bhsd->bhvd', w_s, vc, kc)
        n_new = decay[..., None] * n + jnp.einsum('bhs,bhsd->bhd', w_s, kc)
        return (C_new, n_new, m_new), h

    init = (jnp.zeros((B, H, dv, dk), jnp.float32), jnp.zeros((B, H, dk), jnp.float32),
            jnp.zeros((B, H), jnp.float32))
    xs = (chunks4(q), chunks4(k), chunks4(v), chunks3(li), chunks3(lf))
    _, hs = lax.scan(step, init, xs)
    return hs.transpose(1, 0, 3, 2, 4).reshape(B, S, H, dv)

def mlstm_mixer(xn, w_in, conv_w, conv_b, b_i, b_f, head_norm, w_out):
    B, S, _ = xn.shape
    H = MLSTM_HEADS
    proj = xn @ w_in
    qk_pre, v, o_pre, gates = jnp.split(proj, [2 * QK_W, 2 * QK_W + V_W, 2 * QK_W + 2 * V_W], axis=-1)
    qk = jax.nn.silu(causal_conv(qk_pre, conv_w, conv_b))
    q = qk[..., :QK_W].reshape(B, S, H, MLSTM_DQK).astype(jnp.float32)
    k = qk[..., QK_W:].reshape(B, S, H, MLSTM_DQK).astype(jnp.float32) * (MLSTM_DQK ** -0.5)
    v = v.reshape(B, S, H, MLSTM_DV).astype(jnp.float32)
    gates = gates.astype(jnp.float32)
    li = gates[..., :H] + b_i.astype(jnp.float32)
    lf = jax.nn.log_sigmoid(gates[..., H:] + b_f.astype(jnp.float32))
    h = mlstm_chunkwise(q, k, v, li, lf)
    h = h * lax.rsqrt(jnp.mean(h * h, axis=-1, keepdims=True) + EPS)
    h = h.reshape(B, S, V_W) * head_norm.astype(jnp.float32)
    h = h * jax.nn.sigmoid(o_pre.astype(jnp.float32))
    return h.astype(xn.dtype) @ w_out

def hier_moe(xn, w_gr, b_gr, w_er, b_er, w_gate, w_up, w_down):
    B, S, D = xn.shape
    T = B * S
    xt = xn.reshape(T, D)
    gl = (xt @ w_gr).astype(jnp.float32) + b_gr.astype(jnp.float32)
    gp = jax.nn.softmax(gl, axis=-1)
    gsel = jnp.argmax(gl, axis=-1)
    pg = jnp.take_along_axis(gp, gsel[:, None], axis=-1)[:, 0]
    el = ((xt @ w_er).astype(jnp.float32) + b_er.astype(jnp.float32)).reshape(T, N_GROUPS, EXPERTS_PER_GROUP)
    el_sel = jnp.take_along_axis(el, gsel[:, None, None], axis=1)[:, 0]
    vals, idx = lax.top_k(el_sel, TOP_K)
    wk = jax.nn.softmax(vals, axis=-1) * pg[:, None]
    eid = gsel[:, None] * EXPERTS_PER_GROUP + idx
    comb = jnp.sum(jax.nn.one_hot(eid, N_EXPERTS, dtype=jnp.float32) * wk[..., None], axis=1)
    comb = comb.astype(xn.dtype)
    y = jnp.zeros((T, D), xn.dtype)
    for g in range(N_GROUPS):
        es = slice(g * EXPERTS_PER_GROUP, (g + 1) * EXPERTS_PER_GROUP)
        hg = jnp.einsum('td,edf->tef', xt, w_gate[es])
        hu = jnp.einsum('td,edf->tef', xt, w_up[es])
        act = jax.nn.silu(hg) * hu * comb[:, es, None]
        y = y + jnp.einsum('tef,efd->td', act, w_down[es])
    return y.reshape(B, S, D)

def setup_inputs(seed: int = 0) -> dict:
    key = jax.random.key(seed)
    ks = jax.random.split(key, 20)
    D = D_MODEL
    f32 = jnp.float32
    nrm = lambda k, shape, s: jax.random.normal(k, shape, f32) * s
    b_f = (jnp.tile(jnp.linspace(3.0, 6.0, MLSTM_HEADS, dtype=f32)[None], (N_MLSTM, 1))
           + nrm(ks[8], (N_MLSTM, MLSTM_HEADS), 0.1))
    return {
        "x": nrm(ks[0], (BATCH, SEQ, D), 1.0),
        "mix_norm": 1.0 + nrm(ks[1], (DEPTH, D), 0.02),
        "pool_w": nrm(ks[2], (N_POOL, POOL_GROUPS, POOL_GC, POOL_GC), POOL_GC ** -0.5),
        "pool_scale": 1.0 + nrm(ks[3], (N_POOL, D), 0.02),
        "w_in": nrm(ks[4], (N_MLSTM, D, IN_W), D ** -0.5),
        "conv_w": nrm(ks[5], (N_MLSTM, CONV_K, 2 * QK_W), CONV_K ** -0.5),
        "conv_b": nrm(ks[6], (N_MLSTM, 2 * QK_W), 0.01),
        "gate_bias_i": nrm(ks[7], (N_MLSTM, MLSTM_HEADS), 0.01),
        "gate_bias_f": b_f,
        "head_norm": 1.0 + nrm(ks[9], (N_MLSTM, V_W), 0.02),
        "w_out": nrm(ks[10], (N_MLSTM, V_W, D), V_W ** -0.5),
        "ffn_norm": 1.0 + nrm(ks[11], (DEPTH, D), 0.02),
        "w_group_router": nrm(ks[12], (DEPTH, D, N_GROUPS), D ** -0.5),
        "b_group_router": nrm(ks[13], (DEPTH, N_GROUPS), 0.01),
        "w_expert_router": nrm(ks[14], (DEPTH, D, N_EXPERTS), D ** -0.5),
        "b_expert_router": nrm(ks[15], (DEPTH, N_EXPERTS), 0.01),
        "w_gate": nrm(ks[16], (DEPTH, N_EXPERTS, D, D_FF_EXPERT), D ** -0.5),
        "w_up": nrm(ks[17], (DEPTH, N_EXPERTS, D, D_FF_EXPERT), D ** -0.5),
        "w_down": nrm(ks[18], (DEPTH, N_EXPERTS, D_FF_EXPERT, D), D_FF_EXPERT ** -0.5),
        "final_norm": 1.0 + nrm(ks[19], (D,), 0.02),
    }

def reference(x, mix_norm, pool_w, pool_scale, w_in, conv_w, conv_b, gate_bias_i, gate_bias_f,
              head_norm, w_out, ffn_norm, w_group_router, b_group_router, w_expert_router,
              b_expert_router, w_gate, w_up, w_down, final_norm):
    h = x
    for i in range(DEPTH):
        j = i // N_MIXERS
        hn = rmsnorm(h, mix_norm[i])
        if i % N_MIXERS == 0:
            h = h + pool_mixer(hn, pool_w[j], pool_scale[j])
        else:
            h = h + mlstm_mixer(hn, w_in[j], conv_w[j], conv_b[j], gate_bias_i[j], gate_bias_f[j],
                                head_norm[j], w_out[j])
        hn = rmsnorm(h, ffn_norm[i])
        h = h + hier_moe(hn, w_group_router[i], b_group_router[i], w_expert_router[i],
                         b_expert_router[i], w_gate[i], w_up[i], w_down[i])
    return rmsnorm(h, final_norm)


_drawn_inputs = setup_inputs


def setup_inputs(seed=0):
    import zlib

    import numpy as np

    out = dict(_drawn_inputs(seed))
    spreads = {}
    factors = {'b_group_router': 7.232,
     'b_expert_router': 19.464,
     'final_norm': 8.014,
     'pool_scale': 3.102,
     'ffn_norm': 3.166}
    for name, (base, spread) in spreads.items():
        noise = np.random.default_rng([zlib.crc32(name.encode()), seed]).standard_normal(out[name].shape)
        drawn = base * np.exp(spread * noise) if base else spread * noise
        out[name] = __import__('jax').numpy.asarray(drawn.astype(out[name].dtype))
    for name, factor in factors.items():
        out[name] = (out[name] * factor).astype(out[name].dtype)
    return out
```

```python
from contextlib import ExitStack

import numpy as np

import concourse.bass as bass
from concourse import mybir

F32 = mybir.dt.float32
I32 = mybir.dt.int32
ALU = mybir.AluOpType
ACT = mybir.ActivationFunctionType
AX = mybir.AxisListType

P = 128
EPS = 1e-6
WINDOWS = (2, 4, 8, 16)
TOP_K = 2
NO_ROW = 1 << 20
FAR = 1e30

BAND_NOW, BAND_PREV, BAND_FIRST = 0, 4, 8
IDENT, BEFORE, ONES = 12, 13, 14
VEC = 15 * P
DESC, ROW0, TILE_NO = VEC, VEC + 16, VEC + 32
CONSTS = VEC + 40


def shape_constants(E, T):
    c = np.zeros((P, CONSTS), np.float32)
    s, t = np.arange(P)[:, None], np.arange(P)[None, :]
    for g, w in enumerate(WINDOWS):
        eye = (s == t).astype(np.float32)
        now = ((s <= t) & (s > t - w)).astype(np.float32)
        count = np.minimum(t + 1, w).astype(np.float32)
        c[:, (BAND_NOW + g) * P:(BAND_NOW + g + 1) * P] = now / np.float32(w) - eye
        c[:, (BAND_PREV + g) * P:(BAND_PREV + g + 1) * P] = (s - P > t - w) / np.float32(w)
        c[:, (BAND_FIRST + g) * P:(BAND_FIRST + g + 1) * P] = now / count - eye
    c[:, IDENT * P:(IDENT + 1) * P] = s == t
    c[:, BEFORE * P:(BEFORE + 1) * P] = s < t
    c[:, ONES * P:(ONES + 1) * P] = 1
    c[:, DESC:DESC + E] = E - np.arange(E)
    c[:, ROW0:ROW0 + E] = T * np.arange(E)
    c[:, TILE_NO:TILE_NO + 8] = np.arange(8)
    NT = T // P
    token = (P * np.arange(NT)[None, :, None] + np.arange(P)[:, None, None])
    entry = np.zeros((P, NT, TOP_K, 2), np.int32)
    entry[..., 0] = TOP_K * token + np.arange(TOP_K)[None, None, :]
    entry[..., 1] = token
    return c, entry.reshape(P, NT * TOP_K * 2)


def build(nc, x, mix_norm, pool_w, pool_scale, ffn_norm, w_group, b_group, w_expert, b_expert,
          w_gate, w_up, w_down, final_norm, consts, entries, out):
    T, D = x.shape
    E, _, F = w_gate.shape
    G = w_group.shape[1]
    EPG = E // G
    NT, ND, NF = T // P, D // P, F // P
    GC = D // len(WINDOWS)
    CPG = GC // P
    HALF = D // 2
    NR = G + E
    RING = 3
    W = ND * F
    OV = TOP_K * T // P - 1
    ROWS = E * T + (OV + 2) * P
    assert (E - 1) % RING == 0 and NF * D == W and HALF == 512 and F == 512 and CPG == 2

    rows_dram = nc.dram_tensor("normed_rows", (T, D), F32, kind="Internal").ap()
    table = nc.dram_tensor("slot_table", (ROWS, 2), I32, kind="Internal").ap()
    parts = nc.dram_tensor("expert_parts", (TOP_K * T, D), F32, kind="Internal").ap()

    with ExitStack() as ctx:
        def sb(name, shape, dt=F32):
            return ctx.enter_context(nc.sbuf_tensor(name, shape, dt))

        def sem(name):
            return ctx.enter_context(nc.semaphore(name))

        bank = [ctx.enter_context(nc.psum_tensor(f"bank{i}", [P, 512], F32)) for i in range(8)]

        ring = sb("ring", [P, RING, 3, W])
        h = sb("h", [P, NT, D])
        gx = sb("gx", [P, D])
        xT = sb("xT", [P, ND, P])
        sil = sb("sil", [P, F])
        act = sb("act", [P, F])
        actT = sb("actT", [P, NF, P])
        yrow = sb("yrow", [P, D])
        fnorm = sb("fnorm", [P, D])
        cst = sb("cst", [P, CONSTS])
        ent = sb("ent", [P, NT, TOP_K, 2], I32)
        wr = sb("wr", [P, ND, NR])
        wrs = sb("wrs", [P, ND, NR])
        mixn = sb("mixn", [P, ND])
        ffnn = sb("ffnn", [P, ND])
        bias = sb("bias", [P, NR])
        empty = sb("empty", [P, 2 * ROWS // P], I32)
        slots = sb("slots", [P, E, 2], I32)
        oslots = sb("oslots", [P, 2], I32)
        ss = sb("ss", [P, 3, NT])
        ms, inv, root, newton = (sb(n, [P, 3, NT]) for n in ("ms", "inv", "root", "newton"))
        rstd = sb("rstd", [P, 3, NT])
        L = sb("L", [P, NT, NR])
        gtmp = sb("gtmp", [P, 4, NT, G])
        gcol = sb("gcol", [P, 10, NT])
        em = sb("em", [P, 2, NT, E])
        etmp = sb("etmp", [P, 2, NT, E])
        oh = sb("oh", [P, TOP_K, NT, E])
        mask = sb("mask", [P, NT, E])
        pos = sb("pos", [P, NT, E])
        rowf = sb("rowf", [P, TOP_K, NT])
        rowi = sb("rowi", [P, TOP_K, NT], I32)
        wk = sb("wk", [P, TOP_K, NT])
        cnt = sb("cnt", [P, 6, E])
        ovc = sb("ovc", [P, 2, OV, E])
        ovf = sb("ovf", [P, 6, 8])
        ovi = sb("ovi", [P, 3, 8], I32)

        xr = ring[:, 2, 0, :].rearrange("p (i d) -> p i d", i=NT)
        poolT = ring[:, 2, 1, :].rearrange("p (j t) -> p j t", j=ND)
        rT = ring[:, 2, 2, :].rearrange("p (j t) -> p j t", j=ND)
        wp = ring[:, 1, 2, 0:ND * GC].rearrange("p (j d) -> p j d", j=ND)
        pscale = ring[:, 1, 2, ND * GC:ND * GC + D]
        junk = ring[:, 1, 2, ND * GC + D:ND * GC + 2 * D]
        part = ring[:, 1, 0:2, :].rearrange("p a (b k d) -> p (a b) k d", b=2, k=TOP_K)

        def block_of(n):
            return cst[:, n * P:(n + 1) * P]

        ident = block_of(IDENT)

        x_loaded = [sem(f"x_loaded{i}") for i in range(NT)]
        consts_loaded = sem("consts_loaded")
        pool_w_loaded = sem("pool_w_loaded")
        small_loaded = sem("small_loaded")
        w_loaded = [[sem(f"w{m}_loaded{s}") for m in "gud"] for s in range(RING)]
        squared = sem("squared")
        dve = sem("dve")
        inv_ready = sem("inv_ready")
        root_ready = sem("root_ready")
        xr_ready = sem("xr_ready")
        band_done = sem("band_done")
        poolT_ready = sem("poolT_ready")
        mix_done = sem("mix_done")
        h_ready = sem("h_ready")
        r_ready = sem("r_ready")
        rows_stored = sem("rows_stored")
        rT_psum = sem("rT_psum")
        rT_ready = sem("rT_ready")
        wrs_ready = sem("wrs_ready")
        logits_done = sem("logits_done")
        diff_ready = sem("diff_ready")
        exp_ready = sem("exp_ready")
        mask_ready = sem("mask_ready")
        pos_done = sem("pos_done")
        rowi_ready = sem("rowi_ready")
        empty_ready = sem("empty_ready")
        table_emptied = sem("table_emptied")
        table_filled = sem("table_filled")
        slots_loaded = sem("slots_loaded")
        gx_cleared = sem("gx_cleared")
        gx_loaded = sem("gx_loaded")
        xT_psum = sem("xT_psum")
        xT_ready = sem("xT_ready")
        gate_done = sem("gate_done")
        up_done = sem("up_done")
        sil_ready = sem("sil_ready")
        act_ready = sem("act_ready")
        actT_psum = sem("actT_psum")
        actT_ready = sem("actT_ready")
        y_psum = sem("y_psum")
        y_ready = sem("y_ready")
        y_stored = sem("y_stored")
        o_plan = sem("o_plan")
        o_w_loaded = sem("o_w_loaded")
        o_slots_loaded = sem("o_slots_loaded")
        o_gx_loaded = sem("o_gx_loaded")
        o_pe = sem("o_pe")
        o_act = sem("o_act")
        o_dve = sem("o_dve")
        o_stored = sem("o_stored")
        part_loaded = [sem(f"part_loaded{i}") for i in range(NT)]
        sum_ready = sem("sum_ready")
        out_ready = sem("out_ready")
        out_stored = sem("out_stored")

        block = ctx.enter_context(nc.Block())

        def weights(e, m):
            src = (w_gate, w_up, w_down)[m]
            return src[e].rearrange("(j p) n -> p j n", p=P)

        def ring_at(s, m):
            return ring[:, s, m, :].rearrange("p (j n) -> p j n", j=(ND, ND, NF)[m])

        @block.sync
        def _(sp):
            for i in range(NT):
                sp.dma_start(h[:, i, :], x[i * P:(i + 1) * P, :]).then_inc(x_loaded[i], 16)
                if i == 0:
                    sp.dma_start(cst[:, :], consts).then_inc(consts_loaded, 16)
            sp.dma_start(wp, pool_w.rearrange("g (c p) d -> p (g c) d", p=P)).then_inc(pool_w_loaded, 16)
            sp.dma_start(pscale, pool_scale.partition_broadcast(P)).then_inc(pool_w_loaded, 16)

            def load(e, s, m):
                sp.dma_start(ring_at(s, m), weights(e, m)).then_inc(w_loaded[s][m], 16)

            for m in range(3):
                load(0, 0, m)
            load(1, 1, 0)
            load(1, 1, 1)
            sp.wait_ge(h_ready, NT)
            sp.wait_ge(squared, 2 * NT)
            load(1, 1, 2)
            sp.wait_ge(rows_stored, 16 * NT)
            sp.wait_ge(rT_psum, 2 * NT)
            load(2, 2, 0)
            load(2, 2, 1)
            sp.wait_ge(logits_done, 1)
            load(2, 2, 2)
            def reload(e, s):
                sp.wait_ge(gate_done, e - (RING - 1))
                load(e, s, 0)
                sp.wait_ge(up_done, e - (RING - 1))
                load(e, s, 1)
                sp.wait_ge(y_psum, e * 2 - 2 * (RING - 1))
                load(e, s, 2)

            with sp.Fori(1, E // RING) as it:
                for s in range(RING):
                    reload(it * RING + s, s)
            reload(E - 1, 0)
            sp.wait_ge(o_plan, 1)
            n_over = sp.value_load(ovi[0:1, 2, 0:1], min_val=0, max_val=OV)
            with sp.If(n_over > 0):
                sp.wait_ge(y_psum, 2 * E)
                with sp.Fori(0, OV) as j:
                    e = sp.value_load(ovi[0:1, 1, bass.ds(j, 1)], min_val=0, max_val=E - 1)
                    sp.wait_ge(o_pe, j * 4)
                    for m in range(3):
                        sp.dma_start(ring_at(0, m), weights(e, m)).then_inc(o_w_loaded, 16)
                sp.wait_ge(o_stored, 16 * OV)
            sp.nop()
            sp.wait_ge(y_stored, 16 * E)
            for i in range(NT):
                sp.dma_start(part[:, i], parts[i * TOP_K * P:(i + 1) * TOP_K * P, :]
                             .rearrange("(p k) d -> p k d", k=TOP_K)).then_inc(part_loaded[i], 16)
            for i in range(NT):
                sp.wait_ge(out_ready, i + 1)
                sp.dma_start(out[i * P:(i + 1) * P, :], h[:, i, :]).then_inc(out_stored, 16)
            sp.wait_ge(out_stored, 16 * NT)

        @block.gpsimd
        def _(pool):
            pool.memset(empty[:, :], NO_ROW).then_inc(empty_ready, 1)
            pool.memset(gx[:, :], 0.0).then_inc(gx_cleared, 1)
            pool.wait_ge(empty_ready, 1)
            pool.dma_start(table.rearrange("(p r) c -> p (r c)", p=P), empty[:, :]).then_inc(table_emptied, 16)
            pool.wait_ge(table_emptied, 16)
            pool.wait_ge(small_loaded, 16 * 8)
            for k in range(TOP_K):
                pool.wait_ge(rowi_ready, k + 1)
                for i in range(NT):
                    pool.indirect_dma_start(
                        table, bass.IndirectOffsetOnAxis(rowi[:, k, i:i + 1], 0), ent[:, i, k, :], None,
                    ).then_inc(table_filled, 16)
            pool.wait_ge(table_filled, 16 * NT * TOP_K)
            pool.dma_start(slots[:, :, :], table[0:E * T, :].rearrange("(e c) w -> c e w", c=T)[0:P])\
                .then_inc(slots_loaded, 16)
            pool.wait_ge(slots_loaded, 16)
            pool.wait_ge(rows_stored, 16 * NT)
            pool.wait_ge(gx_cleared, 1)

            def gather(index, done):
                pool.indirect_dma_start(gx[:, :], None, rows_dram, bass.IndirectOffsetOnAxis(index, 0),
                                        bounds_check=T - 1, oob_is_err=False).then_inc(done, 16)

            def scatter(index, done):
                pool.indirect_dma_start(parts, bass.IndirectOffsetOnAxis(index, 0), yrow[:, :], None,
                                        bounds_check=TOP_K * T - 1, oob_is_err=False).then_inc(done, 16)

            gather(slots[:, 0, 1:2], gx_loaded)
            pool.wait_ge(xT_psum, 2)
            gather(slots[:, 1, 1:2], gx_loaded)
            for e in range(E):
                if e + 2 < E:
                    pool.wait_ge(xT_psum, 2 * (e + 2))
                    gather(slots[:, e + 2, 1:2], gx_loaded)
                if e:
                    pool.wait_ge(y_ready, 2 * e)
                    scatter(slots[:, e - 1, 0:1], y_stored)
            pool.wait_ge(y_ready, 2 * E)
            scatter(slots[:, E - 1, 0:1], y_stored)

            pool.wait_ge(o_plan, 1)
            n_over = pool.value_load(ovi[0:1, 2, 0:1], min_val=0, max_val=OV)
            with pool.If(n_over > 0):
                pool.wait_ge(y_stored, 16 * E)
                for j in range(OV):
                    row = pool.value_load(ovi[0:1, 0, j:j + 1], min_val=0, max_val=ROWS - P)
                    pool.dma_start(oslots[:, :], table[bass.ds(row, P), :]).then_inc(o_slots_loaded, 16)
                    pool.wait_ge(o_slots_loaded, j * 16 + 16)
                    gather(oslots[:, 1:2], o_gx_loaded)
                    pool.wait_ge(o_act, j * 4 + 4)
                    scatter(oslots[:, 0:1], o_stored)
                    pool.wait_ge(o_stored, j * 16 + 16)
            pool.nop()

        @block.scalar
        def _(actv):
            for dst, src in ((mixn[:, :], mix_norm),
                             (ffnn[:, :], ffn_norm),
                             (wr[:, :, 0:G], w_group.rearrange("(j p) n -> p j n", p=P)),
                             (wr[:, :, G:NR], w_expert.rearrange("(j p) n -> p j n", p=P)),
                             (bias[:, 0:G], b_group.partition_broadcast(P)),
                             (bias[:, G:NR], b_expert.partition_broadcast(P)),
                             (fnorm[:, :], final_norm.partition_broadcast(P)),
                             (ent[:, :, :, :].rearrange("p i k w -> p (i k w)"), entries)):
                actv.dma_start(dst, src).then_inc(small_loaded, 16)
            for i in range(NT):
                actv.wait_ge(x_loaded[i], 16)
                if i:
                    actv.wait_ge(squared, i)
                actv.activation(junk, h[:, i, :], ACT.Square, accum_out=ss[:, 0, i:i + 1]).then_inc(squared, 1)

            def square_root(n):
                actv.wait_ge(inv_ready, n + 1)
                actv.activation(root[:, n], inv[:, n], ACT.Sqrt).then_inc(root_ready, 1)

            square_root(0)
            actv.wait_ge(small_loaded, 16 * 8)
            for j in range(ND):
                actv.wait_ge(band_done, j + 1)
                actv.activation(poolT[:, j, :], bank[j % 2][:, :], ACT.Copy, scale=mixn[:, j:j + 1])\
                    .then_inc(poolT_ready, 1)
            for i in range(NT):
                actv.wait_ge(h_ready, i + 1)
                actv.wait_ge(squared, NT + i)
                actv.activation(junk, h[:, i, :], ACT.Square, accum_out=ss[:, 1, i:i + 1]).then_inc(squared, 1)
            square_root(1)
            for i in range(NT):
                actv.wait_ge(r_ready, i + 1)
                actv.dma_start(rows_dram[i * P:(i + 1) * P, :], xr[:, i, :]).then_inc(rows_stored, 16)
            for i in range(NT):
                for b in range(2):
                    actv.wait_ge(rT_psum, 2 * i + b + 1)
                    actv.activation(rT[:, 4 * b:4 * b + 4, i * P:(i + 1) * P],
                                    bank[6 + b][:, :].rearrange("p (j t) -> p j t", j=4), ACT.Copy)\
                        .then_inc(rT_ready, 1)
            actv.wait_ge(diff_ready, 1)
            actv.activation(gtmp[:, 1], gtmp[:, 0], ACT.Exp).then_inc(exp_ready, 1)
            actv.wait_ge(diff_ready, 2)
            actv.activation(gcol[:, 7], gcol[:, 6], ACT.Exp).then_inc(exp_ready, 1)

            def step(e, first):
                actv.wait_ge(gate_done, e + 1)
                if not first:
                    actv.wait_ge(act_ready, e)
                actv.activation(sil[:, :], bank[0][:, :], ACT.Silu).then_inc(sil_ready, 1)
                if not first:
                    actv.wait_ge(y_stored, (e - 1) * 16)
                    for b in range(2):
                        actv.wait_ge(y_psum, e * 2 - 1 + b)
                        actv.activation(yrow[:, b * HALF:(b + 1) * HALF], bank[5 + b][:, :], ACT.Copy)\
                            .then_inc(y_ready, 1)
                actv.wait_ge(actT_psum, e + 1)
                actv.activation(actT[:, :, :], bank[4][:, :].rearrange("p (j t) -> p j t", j=NF), ACT.Copy)\
                    .then_inc(actT_ready, 1)

            step(0, True)
            with actv.Fori(0, (E - 1) // RING) as it:
                for s in range(RING):
                    step(it * RING + (1 + s), False)
            actv.wait_ge(y_stored, (E - 1) * 16)
            for b in range(2):
                actv.wait_ge(y_psum, E * 2 - 1 + b)
                actv.activation(yrow[:, b * HALF:(b + 1) * HALF], bank[5 + b][:, :], ACT.Copy).then_inc(y_ready, 1)

            actv.wait_ge(o_plan, 1)
            n_over = actv.value_load(ovi[0:1, 2, 0:1], min_val=0, max_val=OV)
            with actv.If(n_over > 0):
                actv.wait_ge(y_stored, E * 16)
                with actv.Fori(0, OV) as j:
                    actv.wait_ge(o_pe, j * 4 + 2)
                    actv.activation(sil[:, :], bank[0][:, :], ACT.Silu).then_inc(o_act, 1)
                    actv.wait_ge(o_pe, j * 4 + 3)
                    actv.activation(actT[:, :, :], bank[4][:, :].rearrange("p (j t) -> p j t", j=NF), ACT.Copy)\
                        .then_inc(o_act, 1)
                    actv.wait_ge(o_pe, j * 4 + 4)
                    for b in range(2):
                        actv.activation(yrow[:, b * HALF:(b + 1) * HALF], bank[5 + b][:, :], ACT.Copy)\
                            .then_inc(o_act, 1)
            actv.nop()
            for i in range(NT):
                actv.wait_ge(sum_ready, i + 1)
                actv.wait_ge(squared, 2 * NT + i)
                actv.activation(yrow[:, :], h[:, i, :], ACT.Square, accum_out=ss[:, 2, i:i + 1]).then_inc(squared, 1)
            square_root(2)

        @block.vector
        def _(v):
            steps = [0]

            def chain(ins):
                steps[0] += 1
                ins.then_inc(dve, 1)
                v.wait_ge(dve, steps[0])

            def rsqrt_mean(n):
                v.wait_ge(squared, (n + 1) * NT)
                chain(v.tensor_scalar(ms[:, n], ss[:, n], 1.0 / D, EPS, ALU.mult, ALU.add))
                v.reciprocal(inv[:, n], ms[:, n]).then_inc(inv_ready, 1)
                v.wait_ge(root_ready, n + 1)
                chain(v.tensor_tensor(newton[:, n], root[:, n], root[:, n], ALU.mult))
                chain(v.tensor_tensor(newton[:, n], newton[:, n], ms[:, n], ALU.mult))
                chain(v.tensor_scalar(newton[:, n], newton[:, n], -0.5, 1.5, ALU.mult, ALU.add))
                chain(v.tensor_tensor(rstd[:, n], newton[:, n], root[:, n], ALU.mult))

            rsqrt_mean(0)
            for i in range(NT):
                v.tensor_scalar(xr[:, i, :], h[:, i, :], rstd[:, 0, i:i + 1], None, ALU.mult).then_inc(xr_ready, 1)
            v.wait_ge(small_loaded, 16 * 8)
            v.tensor_tensor(wrs[:, :, :], wr[:, :, :], ffnn[:, :].unsqueeze(2).to_broadcast([P, ND, NR]),
                            ALU.mult).then_inc(wrs_ready, 1)
            v.wait_ge(pool_w_loaded, 32)
            for i in range(NT):
                v.wait_ge(mix_done, i + 1)
                for b in range(2):
                    cols = slice(b * HALF, (b + 1) * HALF)
                    if i:
                        v.wait_ge(h_ready, i)
                    chain(v.tensor_tensor(yrow[:, cols], bank[2 + 2 * (i % 2) + b][:, :], pscale[:, cols], ALU.mult))
                ins = v.tensor_tensor(h[:, i, :], h[:, i, :], yrow[:, :], ALU.add)
                ins.then_inc(h_ready, 1)
            rsqrt_mean(1)
            v.wait_ge(band_done, ND)
            for i in range(NT):
                v.tensor_scalar(xr[:, i, :], h[:, i, :], rstd[:, 1, i:i + 1], None, ALU.mult).then_inc(r_ready, 1)

            v.wait_ge(logits_done, 1)
            chain(v.tensor_tensor(L[:, :, :], bank[0][:, 0:NT * NR].rearrange("p (i n) -> p i n", i=NT),
                                  bias[:, :].unsqueeze(1).to_broadcast([P, NT, NR]), ALU.add))
            gl, el = L[:, :, 0:G], L[:, :, G:NR]

            def wide(col, n):
                return col.unsqueeze(2).to_broadcast([P, NT, n])

            def first_largest(vals, n, top, tmp, one_hot, rank):
                chain(v.tensor_tensor(tmp, vals, wide(top, n), ALU.is_equal))
                chain(v.tensor_tensor(tmp, tmp, cst[:, DESC + E - n:DESC + E].unsqueeze(1)
                                      .to_broadcast([P, NT, n]), ALU.mult))
                chain(v.tensor_reduce(rank, tmp, AX.X, ALU.max))
                chain(v.tensor_tensor(one_hot, tmp, wide(rank, n), ALU.is_equal))

            chain(v.tensor_reduce(gcol[:, 0], gl, AX.X, ALU.max))
            v.tensor_tensor(gtmp[:, 0], gl, wide(gcol[:, 0], G), ALU.subtract).then_inc(diff_ready, 1)
            first_largest(gl, G, gcol[:, 0], gtmp[:, 2], gtmp[:, 3], gcol[:, 1])
            chain(v.tensor_scalar(gtmp[:, 2], gtmp[:, 3], FAR, -FAR, ALU.mult, ALU.add))
            for i in range(NT):
                ins = v.tensor_tensor(em[:, 0, i].rearrange("p (g e) -> p g e", g=G),
                                      el[:, i].rearrange("p (g e) -> p g e", g=G),
                                      gtmp[:, 2, i].unsqueeze(2).to_broadcast([P, G, EPG]), ALU.add)
            chain(ins)
            chain(v.tensor_reduce(gcol[:, 2], em[:, 0], AX.X, ALU.max))
            first_largest(em[:, 0], E, gcol[:, 2], etmp[:, 0], oh[:, 0], gcol[:, 3])
            chain(v.scalar_tensor_tensor(em[:, 1], oh[:, 0], -3 * FAR, em[:, 0], ALU.mult, ALU.add))
            chain(v.tensor_reduce(gcol[:, 4], em[:, 1], AX.X, ALU.max))
            first_largest(em[:, 1], E, gcol[:, 4], etmp[:, 1], oh[:, 1], gcol[:, 5])
            v.tensor_tensor(mask[:, :, :], oh[:, 0], oh[:, 1], ALU.add).then_inc(mask_ready, 1)
            v.tensor_tensor(gcol[:, 6], gcol[:, 4], gcol[:, 2], ALU.subtract).then_inc(diff_ready, 1)

            v.wait_ge(pos_done, 1)
            v.tensor_copy(cnt[:, 0], bank[1][:, NT * E:NT * E + E])
            chain(v.tensor_tensor(pos[:, :, :], bank[1][:, 0:NT * E].rearrange("p (i e) -> p i e", i=NT),
                                  cst[:, ROW0:ROW0 + E].unsqueeze(1).to_broadcast([P, NT, E]), ALU.add))
            for k in range(TOP_K):
                chain(v.tensor_tensor(etmp[:, k], oh[:, k], pos[:, :, :], ALU.mult))
                chain(v.tensor_reduce(rowf[:, k], etmp[:, k], AX.X, ALU.add))
                v.tensor_copy(rowi[:, k], rowf[:, k]).then_inc(rowi_ready, 1)

            v.wait_ge(exp_ready, 2)
            chain(v.tensor_reduce(gcol[:, 8], gtmp[:, 1], AX.X, ALU.add))
            chain(v.scalar_tensor_tensor(gcol[:, 9], gcol[:, 7], 1.0, gcol[:, 8], ALU.add, ALU.mult))
            chain(v.reciprocal(wk[:, 0], gcol[:, 9]))
            chain(v.tensor_tensor(wk[:, 1], wk[:, 0], gcol[:, 7], ALU.mult))

            def rows_to_sbuf(b):
                return v.tensor_tensor(xT[:, 4 * b:4 * b + 4, :], bank[2 + b][:, :].rearrange("p (j t) -> p j t", j=4),
                                       ffnn[:, 4 * b:4 * b + 4].unsqueeze(2).to_broadcast([P, 4, P]), ALU.mult)

            for b in range(2):
                v.wait_ge(xT_psum, b + 1)
                rows_to_sbuf(b).then_inc(xT_ready, 1)

            chain(v.memset(cnt[:, 1], 0.0))
            for n in range(1, NT):
                chain(v.scalar_tensor_tensor(cnt[:, 1], cnt[:, 0], float(n * P), cnt[:, 1], ALU.is_gt, ALU.add))
            src = 1
            for n in range(4):
                dst = 2 + n % 2
                d = 1 << n
                v.tensor_copy(cnt[:, dst, 0:d], cnt[:, src, 0:d])
                chain(v.tensor_tensor(cnt[:, dst, d:E], cnt[:, src, d:E], cnt[:, src, 0:E - d], ALU.add))
                src = dst
            total = cnt[:, src]
            chain(v.tensor_tensor(ovc[:, 0], total.unsqueeze(1).to_broadcast([P, OV, E]),
                                  cst[:, TILE_NO:TILE_NO + OV].unsqueeze(2).to_broadcast([P, OV, E]), ALU.is_le))
            chain(v.tensor_reduce(ovf[:, 0, 0:OV], ovc[:, 0], AX.X, ALU.add))
            chain(v.tensor_tensor(ovc[:, 1], ovc[:, 0], cnt[:, 1].unsqueeze(1).to_broadcast([P, OV, E]), ALU.mult))
            chain(v.tensor_reduce(ovf[:, 1, 0:OV], ovc[:, 1], AX.X, ALU.add))
            chain(v.tensor_tensor(ovf[:, 2, 0:OV], cst[:, TILE_NO:TILE_NO + OV], ovf[:, 1, 0:OV], ALU.subtract))
            chain(v.tensor_scalar(ovf[:, 3, 0:OV], ovf[:, 2, 0:OV], 1.0, float(P), ALU.add, ALU.mult))
            chain(v.scalar_tensor_tensor(ovf[:, 4, 0:OV], ovf[:, 0, 0:OV], float(T), ovf[:, 3, 0:OV], ALU.mult, ALU.add))
            v.tensor_copy(ovi[:, 0, 0:OV], ovf[:, 4, 0:OV])
            chain(v.tensor_scalar(ovf[:, 5, 0:OV], ovf[:, 0, 0:OV], float(E - 1), None, ALU.min))
            v.tensor_copy(ovi[:, 1, 0:OV], ovf[:, 5, 0:OV])
            chain(v.tensor_copy(ovi[:, 2, 0:1], total[:, E - 1:E]))
            v.engine_nop().then_inc(o_plan, 1)

            def step(e, last):
                v.wait_ge(sil_ready, e + 1)
                v.wait_ge(up_done, e + 1)
                v.wait_ge(actT_psum, e)
                v.tensor_tensor(act[:, :], sil[:, :], bank[1][:, :], ALU.mult).then_inc(act_ready, 1)
                if not last:
                    for b in range(2):
                        v.wait_ge(xT_psum, e * 2 + (3 + b))
                        rows_to_sbuf(b).then_inc(xT_ready, 1)

            with v.Fori(0, E - 1) as e:
                step(e, False)
            step(E - 1, True)

            n_over = v.value_load(ovi[0:1, 2, 0:1], min_val=0, max_val=OV)
            with v.If(n_over > 0):
                with v.Fori(0, OV) as j:
                    v.wait_ge(o_pe, j * 4 + 1)
                    rows_to_sbuf(0)
                    rows_to_sbuf(1).then_inc(o_dve, 1)
                    v.wait_ge(o_act, j * 4 + 1)
                    v.tensor_tensor(act[:, :], sil[:, :], bank[1][:, :], ALU.mult).then_inc(o_dve, 1)
            v.nop()

            for i in range(NT):
                v.wait_ge(part_loaded[i], 16)
                for k in range(TOP_K):
                    ins = v.scalar_tensor_tensor(h[:, i, :], part[:, i, k, :], wk[:, k, i:i + 1], h[:, i, :],
                                                 ALU.mult, ALU.add)
                    if k == 0:
                        chain(ins)
                    else:
                        ins.then_inc(sum_ready, 1)
            rsqrt_mean(2)
            for i in range(NT):
                v.scalar_tensor_tensor(h[:, i, :], h[:, i, :], rstd[:, 2, i:i + 1], fnorm[:, :],
                                       ALU.mult, ALU.mult).then_inc(out_ready, 1)

        @block.tensor
        def _(pe):
            pe.wait_ge(consts_loaded, 16)
            pe.wait_ge(xr_ready, NT)
            for j in range(ND):
                if j >= 2:
                    pe.wait_ge(poolT_ready, j - 1)
                g = j // CPG
                for i in range(NT):
                    dst = bank[j % 2][:, i * P:(i + 1) * P]
                    cols = slice(j * P, (j + 1) * P)
                    last = pe.matmul(dst, xr[:, i, cols], block_of((BAND_NOW if i else BAND_FIRST) + g),
                                     start=True, stop=(i == 0))
                    if i:
                        last = pe.matmul(dst, xr[:, i - 1, cols], block_of(BAND_PREV + g), start=False, stop=True)
                last.then_inc(band_done, 1)
            pe.wait_ge(pool_w_loaded, 32)
            pe.wait_ge(poolT_ready, ND)
            for i in range(NT):
                if i >= 2:
                    pe.wait_ge(h_ready, i - 1)
                for g in range(len(WINDOWS)):
                    dst = bank[2 + 2 * (i % 2) + g // 2][:, (g % 2) * GC:(g % 2 + 1) * GC]
                    for c in range(CPG):
                        j = g * CPG + c
                        last = pe.matmul(dst, poolT[:, j, i * P:(i + 1) * P], wp[:, j, :],
                                         start=(c == 0), stop=(c == CPG - 1))
                last.then_inc(mix_done, 1)
            for i in range(NT):
                pe.wait_ge(r_ready, i + 1)
                if i:
                    pe.wait_ge(rT_ready, 2 * i)
                for b in range(2):
                    for j in range(4):
                        last = pe.transpose(bank[6 + b][:, j * P:(j + 1) * P],
                                            xr[:, i, (4 * b + j) * P:(4 * b + j + 1) * P], ident)
                    last.then_inc(rT_psum, 1)
            pe.wait_ge(rT_ready, 2 * NT)
            pe.wait_ge(wrs_ready, 1)
            for i in range(NT):
                for j in range(ND):
                    last = pe.matmul(bank[0][:, i * NR:(i + 1) * NR], rT[:, j, i * P:(i + 1) * P], wrs[:, j, :],
                                     start=(j == 0), stop=(j == ND - 1))
            last.then_inc(logits_done, 1)
            pe.wait_ge(mask_ready, 1)
            for i in range(NT + 1):
                dst = bank[1][:, i * E:(i + 1) * E]
                for n in range(min(i, NT)):
                    last = pe.matmul(dst, block_of(ONES), mask[:, n, :], start=(n == 0), stop=(n == NT - 1))
                if i < NT:
                    last = pe.matmul(dst, block_of(BEFORE), mask[:, i, :], start=(i == 0), stop=True)
            last.then_inc(pos_done, 1)

            def rows_transposed():
                for b in range(2):
                    for j in range(4):
                        n = 4 * b + j
                        last = pe.transpose(bank[2 + b][:, j * P:(j + 1) * P], gx[:, n * P:(n + 1) * P], ident)
                    yield last

            def act_transposed():
                for j in range(NF):
                    last = pe.transpose(bank[4][:, j * P:(j + 1) * P], act[:, j * P:(j + 1) * P], ident)
                return last

            def up_or_gate(m, s):
                w = ring_at(s, m)
                for j in range(ND):
                    last = pe.matmul(bank[m][:, :], xT[:, j, :], w[:, j, :], start=(j == 0), stop=(j == ND - 1))
                return last

            def down(b, s):
                w = ring_at(s, 2)
                for j in range(NF):
                    last = pe.matmul(bank[5 + b][:, :], actT[:, j, :], w[:, j, b * HALF:(b + 1) * HALF],
                                     start=(j == 0), stop=(j == NF - 1))
                return last

            def step(e, s, sb_, turn, turn_before, first=False, more=True):
                pe.wait_ge(xT_ready, e * 2 + 2)
                pe.wait_ge(w_loaded[s][0], turn)
                up_or_gate(0, s).then_inc(gate_done, 1)
                pe.wait_ge(w_loaded[s][1], turn)
                up_or_gate(1, s).then_inc(up_done, 1)
                if more:
                    pe.wait_ge(gx_loaded, e * 16 + 32)
                    for last in rows_transposed():
                        last.then_inc(xT_psum, 1)
                if not first:
                    pe.wait_ge(actT_ready, e)
                    pe.wait_ge(w_loaded[sb_][2], turn_before)
                    pe.wait_ge(y_ready, e * 2 - 2)
                    for b in range(2):
                        down(b, sb_).then_inc(y_psum, 1)
                pe.wait_ge(act_ready, e + 1)
                act_transposed().then_inc(actT_psum, 1)

            pe.wait_ge(gx_loaded, 16)
            for last in rows_transposed():
                last.then_inc(xT_psum, 1)
            step(0, 0, 0, 16, 0, first=True)
            with pe.Fori(0, (E - 1) // RING - 1) as it:
                step(it * RING + 1, 1, 0, it * 16 + 16, it * 16 + 16)
                step(it * RING + 2, 2, 1, it * 16 + 16, it * 16 + 16)
                step(it * RING + 3, 0, 2, it * 16 + 32, it * 16 + 16)
            n = (E - 1) // RING - 1
            step(n * RING + 1, 1, 0, n * 16 + 16, n * 16 + 16)
            step(n * RING + 2, 2, 1, n * 16 + 16, n * 16 + 16)
            step(n * RING + 3, 0, 2, n * 16 + 32, n * 16 + 16, more=False)
            pe.wait_ge(actT_ready, E)
            pe.wait_ge(w_loaded[0][2], n * 16 + 32)
            pe.wait_ge(y_ready, 2 * E - 2)
            for b in range(2):
                down(b, 0).then_inc(y_psum, 1)

            pe.wait_ge(o_plan, 1)
            n_over = pe.value_load(ovi[0:1, 2, 0:1], min_val=0, max_val=OV)
            with pe.If(n_over > 0):
                pe.wait_ge(y_ready, 2 * E)
                with pe.Fori(0, OV) as j:
                    pe.wait_ge(o_gx_loaded, j * 16 + 16)
                    for last in rows_transposed():
                        pass
                    last.then_inc(o_pe, 1)
                    pe.wait_ge(o_dve, j * 2 + 1)
                    pe.wait_ge(o_w_loaded, j * 48 + 48)
                    up_or_gate(0, 0)
                    up_or_gate(1, 0).then_inc(o_pe, 1)
                    pe.wait_ge(o_dve, j * 2 + 2)
                    act_transposed().then_inc(o_pe, 1)
                    pe.wait_ge(o_act, j * 4 + 2)
                    down(0, 0)
                    down(1, 0).then_inc(o_pe, 1)
            pe.nop()


_NAMES = ["x", "mix_norm", "pool_w", "pool_scale", "ffn_norm", "w_group_router", "b_group_router",
          "w_expert_router", "b_expert_router", "w_gate", "w_up", "w_down", "final_norm"]


def kernel(**inputs):
    import concourse.bacc as bacc
    from concourse.bass_utils import run_bass_kernel_spmd

    arrays = {}
    for name in _NAMES:
        a = np.ascontiguousarray(inputs[name])
        arrays[name] = a if name == "final_norm" else a.reshape(a.shape[1:])
    for name in ("mix_norm", "ffn_norm"):
        arrays[name] = np.ascontiguousarray(arrays[name].reshape(-1, P).T)
    E, T = arrays["w_gate"].shape[0], arrays["x"].shape[0]
    arrays["consts"], arrays["entries"] = shape_constants(E, T)
    nc = bacc.Bacc("TRN2", target_bir_lowering=False, num_devices=1)
    maps, aps = {}, []
    for name, a in arrays.items():
        maps[f"in_{name}"] = a
        aps.append(nc.dram_tensor(f"in_{name}", a.shape, mybir.dt.from_np(a.dtype), kind="ExternalInput").ap())
    aps.append(nc.dram_tensor("out", arrays["x"].shape, F32, kind="ExternalOutput").ap())
    build(nc, *aps)
    r = run_bass_kernel_spmd(nc, [maps], core_ids=[0])
    return r.results[0]["out"].reshape(inputs["x"].shape)
```

```python
from contextlib import ExitStack

import numpy as np

import concourse.bass as bass
from concourse import mybir

F32 = mybir.dt.float32
F32R = mybir.dt.float32r
F16 = mybir.dt.float16
I32 = mybir.dt.int32
ALU = mybir.AluOpType
ACT = mybir.ActivationFunctionType
AX = mybir.AxisListType

P = 128
EPS = 1e-6
WINDOWS = (2, 4, 8, 16)
TOP_K = 2
FAR = 1e30

FAR_ROW = 2048

BAND_NOW, BAND_PREV, BAND_FIRST, BANDS = 0, 4, 8, 12
IDENT, BEFORE, ONES, SLOT = 0, 1, 2, 3
VEC = 4 * P
DESC, TILE_NO, PAIR, TOKEN = VEC, VEC + 16, VEC + 24, VEC + 28
CONSTS = VEC + 32


def shape_constants(E, T):
    bands = np.zeros((P, BANDS, P), np.float32)
    s, t = np.arange(P)[:, None], np.arange(P)[None, :]
    for g, w in enumerate(WINDOWS):
        eye = (s == t).astype(np.float32)
        now = ((s <= t) & (s > t - w)).astype(np.float32)
        bands[:, BAND_NOW + g] = now / np.float32(w) - eye
        bands[:, BAND_PREV + g] = (s - P > t - w) / np.float32(w)
        bands[:, BAND_FIRST + g] = now / np.minimum(t + 1, w).astype(np.float32) - eye
    c = np.zeros((P, CONSTS), np.float32)
    for n, block in ((IDENT, s == t), (BEFORE, s < t), (ONES, s >= 0), (SLOT, t)):
        c[:, n * P:(n + 1) * P] = block
    c[:, DESC:DESC + E] = E - np.arange(E)
    c[:, TILE_NO:TILE_NO + 8] = np.arange(8)
    for i in range(T // P):
        c[:, PAIR + i] = TOP_K * (i * P + np.arange(P)) - FAR_ROW
        c[:, TOKEN + i] = i * P + np.arange(P) - FAR_ROW
    return bands.reshape(P, BANDS * P), c


def build(nc, x, x_t, mix_norm, pool_w, pool_scale, ffn_norm, ffn_norm_t, w_group, b_group, w_expert, b_expert,
          w_gate, w_up, w_down, final_norm, bands, consts, out):
    T, D = x.shape
    E, _, F = w_gate.shape
    G = w_group.shape[1]
    EPG = E // G
    NT, ND, NF = T // P, D // P, F // P
    GC = D // len(WINDOWS)
    CPG = GC // P
    HALF = D // 2
    NR = G + E
    W = ND * F
    CHUNKS = 4
    C = W // CHUNKS
    BUFS = 4
    STEP = 3 * CHUNKS
    OV = TOP_K * T // P - 1
    assert E % 2 == 0 and NF * D == W and HALF == 512 and F == 512 and CPG == 2 and C == 2 * F == D
    LAST_BANK = 2
    DVE_HOTS = 6
    STEP0_HOTS = 12
    assert TOP_K * T <= FAR_ROW // 2 and BUFS == CHUNKS

    rows_dram = nc.dram_tensor("normed_rows", (T, D), F32, kind="Internal").ap()
    parts = nc.dram_tensor("expert_parts", (TOP_K * T, D), F32, kind="Internal").ap()

    with ExitStack() as ctx:
        def sb(name, shape, dt=F32):
            return ctx.enter_context(nc.sbuf_tensor(name, shape, dt))

        def sem(name):
            return ctx.enter_context(nc.semaphore(name))

        bank = [ctx.enter_context(nc.psum_tensor(f"bank{i}", [P, 512], F32)) for i in range(8)]

        raw = sb("raw", [P, 2, 3, W])
        w_hi = sb("w_hi", [P, BUFS, C], F32R)
        w_lo = sb("w_lo", [P, BUFS, C], F32R)
        h = sb("h", [P, NT, D])
        gx = sb("gx", [P, D])
        x_hi = sb("x_hi", [P, ND, P], F32R)
        x_lo = sb("x_lo", [P, ND, P], F32R)
        sil = sb("sil", [P, F])
        act = sb("act", [P, F])
        act_hi = sb("act_hi", [P, NF, P], F32R)
        act_lo = sb("act_lo", [P, NF, P], F32R)
        yrow = sb("yrow", [P, D])
        fnorm = sb("fnorm", [P, D])
        cst = sb("cst", [P, CONSTS])
        band_hi = sb("band_hi", [P, BANDS, P], F32R)
        band_lo = sb("band_lo", [P, len(WINDOWS), P], F32R)
        count_by = sb("count_by", [P, 2, P], F16)
        wr = sb("wr", [P, ND, NR])
        mixn = sb("mixn", [P, ND])
        ffnn = sb("ffnn", [P, ND])
        bias = sb("bias", [P, NR])
        ss = sb("ss", [P, 3, NT])
        ms, inv, root, newton, rstd = (sb(n, [P, 3, NT]) for n in ("ms", "inv", "root", "newton", "rstd"))
        L = sb("L", [P, NT, NR])
        gtmp = sb("gtmp", [P, 4, NT, G])
        gcol = sb("gcol", [P, 10, NT])
        em = sb("em", [P, 2, NT, E])
        etmp = sb("etmp", [P, 2, NT, E])
        oh = sb("oh", [P, TOP_K, NT, E])
        mask = sb("mask", [P, NT + 1, E], F16)
        pos = sb("pos", [P, 2, NT, E])
        value = sb("value", [P, NT, E, 2], F16)
        onehot = sb("onehot", [P, E, NT, P], F16)
        slots = sb("slots", [P, E, 2], I32)
        oslots = sb("oslots", [P, 2], I32)
        wk = sb("wk", [P, TOP_K, NT])
        cnt = sb("cnt", [P, 4, E])
        cmax = sb("cmax", [P, 2])
        over = sb("over", [P, 1], I32)
        ovc = sb("ovc", [P, 3, OV, E])
        ovf = sb("ovf", [P, 4, 8])
        opos = sb("opos", [P, 3, NT, OV])
        ovalue = sb("ovalue", [P, NT, OV, 2], F16)
        expert_no = sb("expert_no", [P, 8], I32)

        xT = raw[:, 1, 0, :].rearrange("p (i j t) -> p i j t", i=NT, j=ND)
        wp = raw[:, 1, 1, 0:ND * GC].rearrange("p (j d) -> p j d", j=ND)
        pscale = raw[:, 1, 1, ND * GC:ND * GC + D]
        rows = raw[:, 1, 2, :].rearrange("p (i d) -> p i d", i=NT)
        ffnb = yrow[:, :]
        band_raw = raw[:, 0, 2, 0:BANDS * P].rearrange("p (n t) -> p n t", n=BANDS)
        hT = xT
        z_hi, z_lo = w_hi, w_lo
        oxT = raw[:, 1, 0, 0:D].rearrange("p (j t) -> p j t", j=ND)
        oactT = raw[:, 1, 0, D:D + F].rearrange("p (j t) -> p j t", j=NF)
        part = raw[:, 1, 0:2, :].rearrange("p a (b k d) -> p (a b) k d", b=2, k=TOP_K)

        def block_of(n):
            return cst[:, n * P:(n + 1) * P]

        ident = block_of(IDENT)

        x_loaded = [sem(f"x_loaded{i}") for i in range(NT)]
        xT_loaded = [sem(f"xT_loaded{i}") for i in range(NT)]
        bands_loaded = sem("bands_loaded")
        pscale_loaded = sem("pscale_loaded")
        ffnb_loaded = sem("ffnb_loaded")
        consts_loaded = sem("consts_loaded")
        pool_w_loaded = [sem(f"pool_w_loaded{a}") for a in range(2)]
        mixn_loaded = sem("mixn_loaded")
        router_loaded = sem("router_loaded")
        fnorm_loaded = sem("fnorm_loaded")
        w_loaded = [[sem(f"w{m}_loaded{s}") for m in "gud"] for s in range(2)]
        squared = sem("squared")
        dve = sem("dve")
        inv_ready = sem("inv_ready")
        root_ready = sem("root_ready")
        rstd_ready = sem("rstd_ready")
        wp_ready = sem("wp_ready")
        wr_ready = sem("wr_ready")
        count_by_ready = sem("count_by_ready")
        z_psum = sem("z_psum")
        z_hi_ready = sem("z_hi_ready")
        z_lo_ready = sem("z_lo_ready")
        band_hi_ready = sem("band_hi_ready")
        band_lo_ready = sem("band_lo_ready")
        mix_done = sem("mix_done")
        h_ready = sem("h_ready")
        hT_psum = sem("hT_psum")
        hT_ready = sem("hT_ready")
        r_ready = sem("r_ready")
        rows_stored = sem("rows_stored")
        logits_done = sem("logits_done")
        diff_ready = sem("diff_ready")
        exp_ready = sem("exp_ready")
        mask_ready = sem("mask_ready")
        pos_done = sem("pos_done")
        onehot_ready = sem("onehot_ready")
        slot_psum = sem("slot_psum")
        slots_ready = sem("slots_ready")
        over_ready = sem("over_ready")
        pool_onehot_ready = sem("pool_onehot_ready")
        gx_cleared = sem("gx_cleared")
        gx_loaded = sem("gx_loaded")
        yrow_free = sem("yrow_free")
        hi_ready = sem("hi_ready")
        lo_ready = sem("lo_ready")
        used = sem("used")
        xT_psum = sem("xT_psum")
        x_hi_ready = sem("x_hi_ready")
        x_lo_ready = sem("x_lo_ready")
        sil_ready = sem("sil_ready")
        act_ready = sem("act_ready")
        actT_psum = sem("actT_psum")
        act_hi_ready = sem("act_hi_ready")
        act_lo_ready = sem("act_lo_ready")
        y_ready = sem("y_ready")
        y_stored = sem("y_stored")
        o_plan = sem("o_plan")
        o_dve_plan = sem("o_dve_plan")
        o_w_loaded = sem("o_w_loaded")
        o_slots_ready = sem("o_slots_ready")
        o_gx_loaded = sem("o_gx_loaded")
        o_pe = sem("o_pe")
        o_act = sem("o_act")
        o_dve = sem("o_dve")
        o_stored = sem("o_stored")
        part_loaded = [sem(f"part_loaded{i}") for i in range(NT)]
        sum_ready = sem("sum_ready")
        out_ready = sem("out_ready")
        out_stored = sem("out_stored")

        block = ctx.enter_context(nc.Block())

        def chunks_before(e):
            return e * STEP - CHUNKS

        GATE, UP, DOWN = range(3)

        def weights(e, m):
            return (w_gate, w_up, w_down)[m][e].rearrange("(j p) n -> p j n", p=P)

        def raw_at(s, m):
            return raw[:, s, m, :].rearrange("p (j n) -> p j n", j=(ND, ND, NF)[m])

        def raw_chunk(s, m, c):
            return raw[:, s, m, c * C:(c + 1) * C]

        def halves(t):
            return [t[:, 4 * b:4 * b + 4, :] for b in range(2)]

        def bank4(n):
            return bank[n][:, :].rearrange("p (j t) -> p j t", j=4)

        @block.sync
        def _(sp):
            for i in range(NT):
                if i < 2:
                    half = slice(i * (ND // 2), (i + 1) * (ND // 2))
                    sp.dma_start(wp[:, half, :], pool_w[2 * i:2 * i + 2].rearrange("g (c p) d -> p (g c) d", p=P))\
                        .then_inc(pool_w_loaded[i], 16)
                sp.dma_start(xT[:, i], x_t[:, i]).then_inc(xT_loaded[i], 16)
                if i == 0:
                    sp.dma_start(raw[:, 0, 2, 0:BANDS * P], bands).then_inc(bands_loaded, 16)
            sp.dma_start(ffnb, ffn_norm.partition_broadcast(P)).then_inc(ffnb_loaded, 16)

            def load(e, s, m):
                sp.dma_start(raw_at(s, m), weights(e, m)).then_inc(w_loaded[s][m], 16)

            load(0, 0, GATE)
            load(0, 0, UP)
            sp.wait_ge(band_hi_ready, 1)
            sp.wait_ge(band_lo_ready, 1)
            load(0, 0, DOWN)
            sp.wait_ge(z_psum, NT)
            load(1, 1, UP)
            sp.wait_ge(logits_done, 1)
            load(1, 1, GATE)
            sp.wait_ge(rows_stored, 16 * NT)
            load(1, 1, DOWN)
            sp.wait_ge(lo_ready, CHUNKS)
            load(2, 0, GATE)
            sp.wait_ge(lo_ready, 2 * CHUNKS)
            load(2, 0, UP)

            def reload(e, s):
                sp.wait_ge(lo_ready, e * STEP - (2 * STEP + CHUNKS) + CHUNKS)
                load(e, s, GATE)
                sp.wait_ge(lo_ready, e * STEP - (2 * STEP + CHUNKS) + 2 * CHUNKS)
                load(e, s, UP)
                sp.wait_ge(lo_ready, e * STEP - (2 * STEP + CHUNKS) + 3 * CHUNKS)
                load(e - 1, 1 - s, DOWN)

            with sp.Fori(1, E // 2 - 1) as it:
                reload(it * 2 + 1, 1)
                reload(it * 2 + 2, 0)
            reload(E - 1, 1)
            sp.wait_ge(lo_ready, chunks_before(E - 2) + 3 * CHUNKS)
            load(E - 1, 1, DOWN)

            sp.wait_ge(over_ready, 1)
            n_over = sp.value_load(over[0:1, 0:1], min_val=0, max_val=T)
            with sp.If(n_over > 0):
                sp.wait_ge(o_plan, 1)
                for j in range(OV):
                    e = sp.value_load(expert_no[0:1, j:j + 1], min_val=0, max_val=E - 1)
                    if j:
                        sp.wait_ge(o_pe, 5 * j)
                    for m in range(3):
                        sp.dma_start(raw_at(0, m), weights(e, m)).then_inc(o_w_loaded, 16)
                sp.wait_ge(o_stored, 16 * OV)
            sp.nop()
            sp.wait_ge(yrow_free, E + 1)
            for i in range(NT):
                sp.dma_start(part[:, i], parts[i * TOP_K * P:(i + 1) * TOP_K * P, :]
                             .rearrange("(p k) d -> p k d", k=TOP_K)).then_inc(part_loaded[i], 16)
            for i in range(NT):
                sp.wait_ge(out_ready, i + 1)
                sp.dma_start(out[i * P:(i + 1) * P, :], h[:, i, :]).then_inc(out_stored, 16)
            sp.wait_ge(out_stored, 16 * NT)

        @block.gpsimd
        def _(pool):
            for dst, src, done in ((mixn[:, :], mix_norm, mixn_loaded),
                                   (cst[:, :], consts, consts_loaded),
                                   (ffnn[:, :], ffn_norm_t, router_loaded),
                                   (wr[:, :, 0:G], w_group.rearrange("(j p) n -> p j n", p=P), router_loaded),
                                   (wr[:, :, G:NR], w_expert.rearrange("(j p) n -> p j n", p=P), router_loaded),
                                   (bias[:, 0:G], b_group.partition_broadcast(P), router_loaded),
                                   (bias[:, G:NR], b_expert.partition_broadcast(P), router_loaded)):
                pool.dma_start(dst, src).then_inc(done, 16)
            pool.memset(gx[:, :], 0.0).then_inc(gx_cleared, 1)
            for i in range(NT):
                pool.wait_ge(r_ready, i + 1)
                pool.dma_start(rows_dram[i * P:(i + 1) * P, :], rows[:, i, :]).then_inc(rows_stored, 16)
            pool.sem_inc(yrow_free, 1)
            pool.wait_ge(rows_stored, 16 * NT)
            pool.wait_ge(gx_cleared, 1)

            def gather(index, done):
                return pool.indirect_dma_start(gx[:, :], None, rows_dram, bass.IndirectOffsetOnAxis(index, 0),
                                               bounds_check=T - 1, oob_is_err=False).then_inc(done, 16)

            def scatter(index, done):
                pool.indirect_dma_start(parts, bass.IndirectOffsetOnAxis(index, 0), yrow[:, :], None,
                                        bounds_check=TOP_K * T - 1, oob_is_err=False).then_inc(done, 16)

            def store_results(e):
                pool.wait_ge(y_ready, 2 * e + 2)
                scatter(slots[:, e, 0:1], y_stored)

            pool.wait_ge(slots_ready, 1)
            gather(slots[:, 0, 1:2], gx_loaded)

            def one_hots(experts):
                for e in experts:
                    for i in range(NT):
                        ins = pool.tensor_scalar(onehot[:, e, i, :], block_of(SLOT), pos[:, 1, i, e:e + 1],
                                                 None, ALU.is_equal)
                    ins.then_inc(pool_onehot_ready, 1)

            one_hots(range(DVE_HOTS, DVE_HOTS + 1))
            pool.wait_ge(xT_psum, 2)
            gather(slots[:, 1, 1:2], gx_loaded)
            one_hots(range(DVE_HOTS + 1, STEP0_HOTS))
            pool.wait_ge(slots_ready, 2)
            pool.wait_ge(xT_psum, 4)
            gather(slots[:, 2, 1:2], gx_loaded)
            one_hots(range(STEP0_HOTS, E))
            for e in range(E):
                if e + 2 < E:
                    if e:
                        if e + 2 == DVE_HOTS:
                            pool.wait_ge(slots_ready, 3)
                        pool.wait_ge(xT_psum, 2 * (e + 2))
                        gather(slots[:, e + 2, 1:2], gx_loaded)
                    if e >= 2:
                        pool.wait_ge(y_stored, 16 * (e - 1))
                        pool.sem_inc(yrow_free, 1)
                if e:
                    if e + 2 >= E:
                        pool.wait_ge(y_stored, 16 * (e - 1))
                        pool.sem_inc(yrow_free, 1)
                    store_results(e - 1)
            pool.wait_ge(y_stored, 16 * (E - 1))
            pool.sem_inc(yrow_free, 1)
            store_results(E - 1)
            pool.wait_ge(y_stored, 16 * E)
            pool.sem_inc(yrow_free, 1)

            pool.wait_ge(over_ready, 1)
            n_over = pool.value_load(over[0:1, 0:1], min_val=0, max_val=T)
            with pool.If(n_over > 0):
                for j in range(OV):
                    pool.wait_ge(o_slots_ready, j + 1)
                    gather(oslots[:, 1:2], o_gx_loaded)
                    pool.wait_ge(o_act, 4 * j + 4)
                    scatter(oslots[:, 0:1], o_stored)
            pool.nop()

        @block.scalar
        def _(actv):
            actv.dma_start(pscale, pool_scale.partition_broadcast(P)).then_inc(pscale_loaded, 16)
            for i in range(NT):
                actv.dma_start(h[:, i, :], x[i * P:(i + 1) * P, :]).then_inc(x_loaded[i], 16)
            actv.wait_ge(gx_cleared, 1)

            def square(n, i):
                if n + i:
                    actv.wait_ge(squared, n * NT + i)
                actv.activation(gx[:, :], h[:, i, :], ACT.Square, accum_out=ss[:, n, i:i + 1]).then_inc(squared, 1)

            def square_root(turn, n, cols):
                actv.wait_ge(inv_ready, turn)
                actv.activation(root[:, n, cols], inv[:, n, cols], ACT.Sqrt).then_inc(root_ready, 1)

            def norm_z(i):
                actv.wait_ge(z_psum, i + 1)
                for b in range(2):
                    cols = slice(b * HALF, (b + 1) * HALF)
                    actv.activation(z_hi[:, i, cols], bank[2 * (i % 2) + b][:, :], ACT.Copy,
                                    scale=rstd[:, 0, i:i + 1]).then_inc(z_hi_ready, 1)

            def copy_hT(i):
                for b in range(2):
                    actv.wait_ge(hT_psum, 2 * i + b + 1)
                    actv.activation(hT[:, i, 4 * b:4 * b + 4, :], bank4(6 + b), ACT.Copy).then_inc(hT_ready, 1)

            def square_h(i):
                actv.wait_ge(h_ready, i + 1)
                square(1, i)

            for i in range(NT):
                actv.wait_ge(x_loaded[i], 16)
                square(0, i)
                if i % 2:
                    square_root((i + 1) // 2, 0, slice(i - 1, i + 1))
            actv.wait_ge(consts_loaded, 16)
            actv.activation(count_by[:, :, :], cst[:, BEFORE * P:(ONES + 1) * P].rearrange("p (n t) -> p n t", n=2),
                            ACT.Copy).then_inc(count_by_ready, 1)
            actv.wait_ge(bands_loaded, 16)
            actv.activation(band_hi[:, :, :], band_raw, ACT.Copy).then_inc(band_hi_ready, 1)
            actv.wait_ge(rstd_ready, 1)
            norm_z(0)
            norm_z(1)
            square_h(0)
            actv.wait_ge(rstd_ready, 2)
            norm_z(2)
            square_h(1)
            copy_hT(0)
            norm_z(3)
            square_root(3, 1, slice(0, 2))
            copy_hT(1)
            square_h(2)
            copy_hT(2)
            square_h(3)
            square_root(4, 1, slice(2, 4))
            copy_hT(3)
            actv.dma_start(fnorm[:, :], final_norm.partition_broadcast(P)).then_inc(fnorm_loaded, 16)
            actv.wait_ge(diff_ready, 1)
            actv.activation(gtmp[:, 1], gtmp[:, 0], ACT.Exp).then_inc(exp_ready, 1)
            actv.wait_ge(diff_ready, 2)
            actv.activation(gcol[:, 7], gcol[:, 6], ACT.Exp).then_inc(exp_ready, 1)
            actv.wait_ge(logits_done, 1)

            def round_chunks(m, s, turn, first_chunk, wait=True):
                actv.wait_ge(w_loaded[s][m], turn)
                for c in range(CHUNKS):
                    if wait:
                        actv.wait_ge(used, first_chunk + (c + 1 - BUFS))
                    actv.activation(w_hi[:, c, :], raw_chunk(s, m, c), ACT.Copy).then_inc(hi_ready, 1)

            def rows_high(e):
                for b, dst in enumerate(halves(x_hi)):
                    actv.wait_ge(xT_psum, e * 2 + (b + 1))
                    actv.activation(dst, bank4(2 + b), ACT.Copy).then_inc(x_hi_ready, 1)

            def act_high(e):
                actv.wait_ge(actT_psum, e + 1)
                actv.activation(act_hi[:, :, :], bank4(4), ACT.Copy).then_inc(act_hi_ready, 1)

            def results(e, first_bank=5):
                actv.wait_ge(yrow_free, e + 1)
                for b in range(2):
                    actv.activation(yrow[:, b * HALF:(b + 1) * HALF], bank[first_bank + b][:, :], ACT.Copy)\
                        .then_inc(y_ready, 1)

            def step(e, s, turn, turn_before, first=False, second=False, last=False):
                n = 0 if first else chunks_before(e)
                round_chunks(GATE, s, turn, n, wait=not first)
                if not first:
                    if not second:
                        results(e - 2)
                    act_high(e - 1)
                round_chunks(UP, s, turn, n + CHUNKS)
                if not first:
                    actv.wait_ge(act_ready, e)
                actv.activation(sil[:, :], bank[0][:, :], ACT.Silu).then_inc(sil_ready, 1)
                if not first:
                    round_chunks(DOWN, 1 - s, turn_before, n + 2 * CHUNKS)
                if not last:
                    rows_high(e + 1)

            rows_high(0)
            step(0, 0, 16, None, first=True)
            step(1, 1, 16, 16, second=True)
            with actv.Fori(1, E // 2 - 1) as it:
                step(it * 2, 0, it * 16 + 16, it * 16)
                step(it * 2 + 1, 1, it * 16 + 16, it * 16 + 16)
            step(E - 2, 0, 8 * E, 8 * E - 16)
            step(E - 1, 1, 8 * E, 8 * E, last=True)
            round_chunks(DOWN, 1, 8 * E, chunks_before(E))
            act_high(E - 1)
            results(E - 2)
            actv.activation(root[:, 2, :], inv[:, 1, :], ACT.Sqrt)
            actv.wait_ge(used, chunks_before(E) + CHUNKS)
            results(E - 1, LAST_BANK)

            actv.wait_ge(over_ready, 1)
            n_over = actv.value_load(over[0:1, 0:1], min_val=0, max_val=T)
            with actv.If(n_over > 0):
                actv.wait_ge(yrow_free, E + 1)
                with actv.Fori(0, OV) as j:
                    actv.wait_ge(o_pe, j * 5 + 3)
                    actv.activation(sil[:, :], bank[0][:, :], ACT.Silu).then_inc(o_act, 1)
                    actv.wait_ge(o_pe, j * 5 + 4)
                    actv.activation(oactT, bank4(4), ACT.Copy).then_inc(o_act, 1)
                    actv.wait_ge(o_pe, j * 5 + 5)
                    for b in range(2):
                        actv.activation(yrow[:, b * HALF:(b + 1) * HALF], bank[5 + b][:, :], ACT.Copy)\
                            .then_inc(o_act, 1)
            actv.nop()
            for i in range(NT):
                actv.wait_ge(sum_ready, i + 1)
                square(2, i)
                square_root(5 + i, 2, slice(i, i + 1))

        @block.vector
        def _(v):
            steps = {"dve": 0, "o_dve_plan": 0}

            def chain(ins, own="dve"):
                done = dve if own == "dve" else o_dve_plan
                steps[own] += 1
                ins.then_inc(done, 1)
                v.wait_ge(done, steps[own])

            def rsqrt_mean(turn, n, cols):
                v.wait_ge(squared, n * NT + cols.stop)
                chain(v.tensor_scalar(ms[:, n, cols], ss[:, n, cols], 1.0 / D, EPS, ALU.mult, ALU.add))
                v.reciprocal(inv[:, n, cols], ms[:, n, cols]).then_inc(inv_ready, 1)
                v.wait_ge(root_ready, turn)
                chain(v.tensor_tensor(newton[:, n, cols], root[:, n, cols], root[:, n, cols], ALU.mult))
                chain(v.tensor_tensor(newton[:, n, cols], newton[:, n, cols], ms[:, n, cols], ALU.mult))
                chain(v.tensor_scalar(newton[:, n, cols], newton[:, n, cols], -0.5, 1.5, ALU.mult, ALU.add))
                return v.tensor_tensor(rstd[:, n, cols], newton[:, n, cols], root[:, n, cols], ALU.mult)

            def rest(dst, src, high):
                return v.tensor_tensor(dst, src, high.bitcast(F32), ALU.subtract)

            v.wait_ge(mixn_loaded, 16)
            v.wait_ge(pscale_loaded, 16)
            for j in range(ND):
                if j % (ND // 2) == 0:
                    v.wait_ge(pool_w_loaded[j // (ND // 2)], 16)
                g = j // CPG
                v.scalar_tensor_tensor(wp[:, j, :], wp[:, j, :], mixn[:, j:j + 1], pscale[:, g * GC:(g + 1) * GC],
                                       ALU.mult, ALU.mult).then_inc(wp_ready, 1)
            for pair in range(NT // 2):
                rsqrt_mean(pair + 1, 0, slice(2 * pair, 2 * pair + 2)).then_inc(rstd_ready, 1)
            v.wait_ge(rstd_ready, NT // 2)
            v.wait_ge(band_hi_ready, 1)
            rest(band_lo[:, :, :], band_raw[:, BAND_FIRST:BANDS], band_hi[:, BAND_FIRST:BANDS]).then_inc(band_lo_ready, 1)

            def z_low(i):
                for b in range(2):
                    v.wait_ge(z_hi_ready, 2 * i + b + 1)
                    cols = slice(b * HALF, (b + 1) * HALF)
                    v.scalar_tensor_tensor(z_lo[:, i, cols], bank[2 * (i % 2) + b][:, :], rstd[:, 0, i:i + 1],
                                           z_hi[:, i, cols].bitcast(F32), ALU.mult, ALU.subtract)\
                        .then_inc(z_lo_ready, 1)

            z_low(0)
            z_low(1)
            v.wait_ge(router_loaded, 80)
            v.tensor_tensor(wr[:, :, :], wr[:, :, :], ffnn[:, :].unsqueeze(2).to_broadcast([P, ND, NR]), ALU.mult)\
                .then_inc(wr_ready, 1)
            v.memset(mask[:, NT, :], 0.0)
            v.wait_ge(ffnb_loaded, 16)
            for i in range(NT):
                v.wait_ge(mix_done, i + 1)
                for b in range(2):
                    cols = slice(b * HALF, (b + 1) * HALF)
                    ins = v.tensor_tensor(h[:, i, cols], bank[4 + b][:, :], h[:, i, cols], ALU.add)
                ins.then_inc(h_ready, 1)
                if i + 2 < NT:
                    z_low(i + 2)
                if i % 2:
                    chain(rsqrt_mean(3 + i // 2, 1, slice(i - 1, i + 1)))
                    for t in (i - 1, i):
                        v.scalar_tensor_tensor(rows[:, t, :], h[:, t, :], rstd[:, 1, t:t + 1], ffnb,
                                               ALU.mult, ALU.mult).then_inc(r_ready, 1)

            v.wait_ge(logits_done, 1)
            chain(v.tensor_tensor(L[:, :, :], bank[0][:, 0:NT * NR].rearrange("p (i n) -> p i n", i=NT),
                                  rstd[:, 1, :].unsqueeze(2).to_broadcast([P, NT, NR]), ALU.mult))
            chain(v.tensor_tensor(L[:, :, :], L[:, :, :], bias[:, :].unsqueeze(1).to_broadcast([P, NT, NR]), ALU.add))
            gl, el = L[:, :, 0:G], L[:, :, G:NR]

            def wide(col, n):
                return col.unsqueeze(2).to_broadcast([P, NT, n])

            def first_largest(vals, n, top, tmp, one_hot, rank):
                chain(v.tensor_tensor(tmp, vals, wide(top, n), ALU.is_equal))
                chain(v.tensor_tensor(tmp, tmp, cst[:, DESC + E - n:DESC + E].unsqueeze(1)
                                      .to_broadcast([P, NT, n]), ALU.mult))
                chain(v.tensor_reduce(rank, tmp, AX.X, ALU.max))
                chain(v.tensor_tensor(one_hot, tmp, wide(rank, n), ALU.is_equal))

            chain(v.tensor_reduce(gcol[:, 0], gl, AX.X, ALU.max))
            v.tensor_tensor(gtmp[:, 0], gl, wide(gcol[:, 0], G), ALU.subtract).then_inc(diff_ready, 1)
            first_largest(gl, G, gcol[:, 0], gtmp[:, 2], gtmp[:, 3], gcol[:, 1])
            chain(v.tensor_scalar(gtmp[:, 2], gtmp[:, 3], FAR, -FAR, ALU.mult, ALU.add))
            for i in range(NT):
                ins = v.tensor_tensor(em[:, 0, i].rearrange("p (g e) -> p g e", g=G),
                                      el[:, i].rearrange("p (g e) -> p g e", g=G),
                                      gtmp[:, 2, i].unsqueeze(2).to_broadcast([P, G, EPG]), ALU.add)
            chain(ins)
            chain(v.tensor_reduce(gcol[:, 2], em[:, 0], AX.X, ALU.max))
            first_largest(em[:, 0], E, gcol[:, 2], etmp[:, 0], oh[:, 0], gcol[:, 3])
            chain(v.scalar_tensor_tensor(em[:, 1], oh[:, 0], -3 * FAR, em[:, 0], ALU.mult, ALU.add))
            chain(v.tensor_reduce(gcol[:, 4], em[:, 1], AX.X, ALU.max))
            first_largest(em[:, 1], E, gcol[:, 4], etmp[:, 1], oh[:, 1], gcol[:, 5])
            v.tensor_tensor(mask[:, 0:NT, :], oh[:, 0], oh[:, 1], ALU.add).then_inc(mask_ready, 1)
            v.tensor_tensor(gcol[:, 6], gcol[:, 4], gcol[:, 2], ALU.subtract).then_inc(diff_ready, 1)
            v.tensor_tensor(value[:, :, :, 0], oh[:, 1], wide(cst[:, PAIR:PAIR + NT], E), ALU.add)
            chain(v.tensor_copy(value[:, :, :, 1], wide(cst[:, TOKEN:TOKEN + NT], E)))

            v.wait_ge(pos_done, 1)
            chain(v.scalar_tensor_tensor(pos[:, 0], bank[1][:, 0:NT * E].rearrange("p (i e) -> p i e", i=NT), 1.0,
                                         mask[:, 0:NT, :], ALU.add, ALU.mult))
            chain(v.tensor_scalar(pos[:, 1], pos[:, 0], -1.0, None, ALU.add))

            def one_hots(experts):
                for e in experts:
                    for i in range(NT):
                        ins = v.tensor_scalar(onehot[:, e, i, :], block_of(SLOT), pos[:, 1, i, e:e + 1], None,
                                              ALU.is_equal)
                    ins.then_inc(onehot_ready, 1)

            one_hots(range(2))
            v.tensor_copy(cnt[:, 0], bank[1][:, NT * E:NT * E + E])

            def slot_numbers(dst, src):
                return v.tensor_scalar(dst, src, float(FAR_ROW), None, ALU.add)

            slot_bank = bank[7][:, 0:2 * E].rearrange("p (e w) -> p e w", w=2)
            v.wait_ge(slot_psum, 2)
            slot_numbers(slots[:, 0:2, :], slot_bank[:, 0:2, :]).then_inc(slots_ready, 1)
            one_hots(range(2, DVE_HOTS))

            v.wait_ge(exp_ready, 2)
            chain(v.tensor_reduce(gcol[:, 8], gtmp[:, 1], AX.X, ALU.add))
            chain(v.scalar_tensor_tensor(gcol[:, 9], gcol[:, 7], 1.0, gcol[:, 8], ALU.add, ALU.mult))
            chain(v.reciprocal(wk[:, 0], gcol[:, 9]))
            chain(v.tensor_tensor(wk[:, 1], wk[:, 0], gcol[:, 7], ALU.mult))
            chain(v.tensor_reduce(cmax[:, 0:1], cnt[:, 0], AX.X, ALU.max))
            chain(v.tensor_scalar(cmax[:, 1:2], cmax[:, 0:1], -float(P), 0.0, ALU.add, ALU.max))
            v.tensor_copy(over[:, :], cmax[:, 1:2]).then_inc(over_ready, 1)
            v.wait_ge(slot_psum, DVE_HOTS)
            slot_numbers(slots[:, 2:DVE_HOTS, :], slot_bank[:, 2:DVE_HOTS, :]).then_inc(slots_ready, 1)

            def rests_of_chunks(m, s, first_chunk, chunks=range(CHUNKS)):
                for c in chunks:
                    v.wait_ge(hi_ready, first_chunk + (c + 1))
                    rest(w_lo[:, c, :], raw_chunk(s, m, c), w_hi[:, c, :]).then_inc(lo_ready, 1)

            def rows_low(e):
                for b, (dst, high) in enumerate(zip(halves(x_lo), halves(x_hi))):
                    v.wait_ge(x_hi_ready, e * 2 + (b + 1))
                    rest(dst, bank4(2 + b), high).then_inc(x_lo_ready, 1)

            def act_low(e):
                v.wait_ge(act_hi_ready, e + 1)
                rest(act_lo[:, :, :], bank4(4), act_hi[:, :, :]).then_inc(act_lo_ready, 1)

            def step(e, s, first=False, second=False, last=False):
                n = 0 if first else chunks_before(e)
                rests_of_chunks(GATE, s, n)
                if not first:
                    act_low(e - 1)
                rests_of_chunks(UP, s, n + CHUNKS)
                if not first:
                    rests_of_chunks(DOWN, 1 - s, n + 2 * CHUNKS, range(CHUNKS - 1))
                v.wait_ge(sil_ready, e + 1)
                v.wait_ge(used, n + 2 * CHUNKS)
                v.tensor_tensor(act[:, :], sil[:, :], bank[1][:, :], ALU.mult).then_inc(act_ready, 1)
                if not first:
                    rests_of_chunks(DOWN, 1 - s, n + 2 * CHUNKS, range(CHUNKS - 1, CHUNKS))
                if not last:
                    rows_low(e + 1)
                if second:
                    v.wait_ge(slot_psum, E)
                    slot_numbers(slots[:, DVE_HOTS:E, :], slot_bank[:, DVE_HOTS:E, :]).then_inc(slots_ready, 1)

            rows_low(0)
            step(0, 0, first=True)
            step(1, 1, second=True)
            with v.Fori(1, E // 2 - 1) as it:
                step(it * 2, 0)
                step(it * 2 + 1, 1)
            step(E - 2, 0)
            step(E - 1, 1, last=True)
            rests_of_chunks(DOWN, 1, chunks_before(E))
            act_low(E - 1)

            n_over = v.value_load(over[0:1, 0:1], min_val=0, max_val=T)
            with v.If(n_over > 0):
                def plan(ins):
                    chain(ins, "o_dve_plan")

                plan(v.memset(cnt[:, 1], 0.0))
                for n in range(1, NT):
                    plan(v.scalar_tensor_tensor(cnt[:, 1], cnt[:, 0], float(n * P), cnt[:, 1], ALU.is_gt, ALU.add))
                src = 1
                for n in range(4):
                    dst = 2 + n % 2
                    d = 1 << n
                    v.tensor_copy(cnt[:, dst, 0:d], cnt[:, src, 0:d])
                    plan(v.tensor_tensor(cnt[:, dst, d:E], cnt[:, src, d:E], cnt[:, src, 0:E - d], ALU.add))
                    src = dst
                over_all = [P, OV, E]
                passed, mine = ovc[:, 0], ovc[:, 2]
                plan(v.tensor_tensor(passed, cnt[:, src].unsqueeze(1).to_broadcast(over_all),
                                      cst[:, TILE_NO:TILE_NO + OV].unsqueeze(2).to_broadcast(over_all), ALU.is_le))
                plan(v.tensor_reduce(ovf[:, 0, 0:OV], passed, AX.X, ALU.add))
                plan(v.tensor_tensor(ovc[:, 1], passed, cnt[:, 1].unsqueeze(1).to_broadcast(over_all), ALU.mult))
                plan(v.tensor_reduce(ovf[:, 1, 0:OV], ovc[:, 1], AX.X, ALU.add))
                plan(v.tensor_tensor(ovf[:, 2, 0:OV], cst[:, TILE_NO:TILE_NO + OV], ovf[:, 1, 0:OV], ALU.subtract))
                plan(v.tensor_scalar(ovf[:, 3, 0:OV], ovf[:, 2, 0:OV], 1.0, float(P), ALU.add, ALU.mult))
                v.tensor_scalar(mine[:, :, 0:1], passed[:, :, 0:1], -1.0, 1.0, ALU.mult, ALU.add)
                plan(v.tensor_tensor(mine[:, :, 1:E], passed[:, :, 0:E - 1], passed[:, :, 1:E], ALU.subtract))
                for i in range(NT):
                    plan(v.tensor_tensor(ovc[:, 1], mine, pos[:, 1, i].unsqueeze(1).to_broadcast(over_all), ALU.mult))
                    plan(v.tensor_reduce(opos[:, 0, i], ovc[:, 1], AX.X, ALU.add))
                    plan(v.tensor_tensor(opos[:, 1, i], opos[:, 0, i], ovf[:, 3, 0:OV], ALU.subtract))
                    plan(v.tensor_tensor(ovc[:, 1], mine, oh[:, 1, i].unsqueeze(1).to_broadcast(over_all), ALU.mult))
                    plan(v.tensor_reduce(opos[:, 2, i], ovc[:, 1], AX.X, ALU.add))
                    v.tensor_scalar(ovalue[:, i, :, 0], opos[:, 2, i], cst[:, PAIR + i:PAIR + i + 1], None, ALU.add)
                    plan(v.tensor_copy(ovalue[:, i, :, 1], cst[:, TOKEN + i:TOKEN + i + 1].to_broadcast([P, OV])))
                plan(v.tensor_scalar(ovf[:, 1, 0:OV], ovf[:, 0, 0:OV], float(E - 1), None, ALU.min))
                v.wait_ge(yrow_free, E + 1)
                v.tensor_copy(expert_no[:, 0:OV], ovf[:, 1, 0:OV]).then_inc(o_plan, 1)
                for j in range(OV):
                    if j:
                        v.wait_ge(o_stored, 16 * j)
                    for i in range(NT):
                        ins = v.tensor_scalar(onehot[:, 0, i, :], block_of(SLOT), opos[:, 1, i, j:j + 1], None,
                                              ALU.is_equal)
                    ins.then_inc(o_dve, 1)
                    v.wait_ge(o_pe, 5 * j + 1)
                    slot_numbers(oslots[:, :], bank[7][:, 0:2]).then_inc(o_slots_ready, 1)
                    v.wait_ge(o_pe, 5 * j + 2)
                    v.tensor_copy(halves(oxT)[0], bank4(2))
                    v.tensor_copy(halves(oxT)[1], bank4(3)).then_inc(o_dve, 1)
                    v.wait_ge(o_act, 4 * j + 1)
                    v.tensor_tensor(act[:, :], sil[:, :], bank[1][:, :], ALU.mult).then_inc(o_dve, 1)
            v.nop()

            v.wait_ge(fnorm_loaded, 16)
            def add_parts(i):
                v.wait_ge(part_loaded[i], 16)
                chain(v.scalar_tensor_tensor(h[:, i, :], part[:, i, 0, :], wk[:, 0, i:i + 1], h[:, i, :],
                                             ALU.mult, ALU.add))
                v.scalar_tensor_tensor(h[:, i, :], part[:, i, 1, :], wk[:, 1, i:i + 1], h[:, i, :],
                                       ALU.mult, ALU.add).then_inc(sum_ready, 1)

            def finish(i):
                chain(rsqrt_mean(5 + i, 2, slice(i, i + 1)))
                v.scalar_tensor_tensor(h[:, i, :], h[:, i, :], rstd[:, 2, i:i + 1], fnorm[:, :],
                                       ALU.mult, ALU.mult).then_inc(out_ready, 1)

            add_parts(0)
            for i in range(1, NT):
                add_parts(i)
                finish(i - 1)
            finish(NT - 1)

        @block.tensor
        def _(pe):
            def project(i):
                pe.wait_ge(xT_loaded[i], 16)
                if i >= 2:
                    pe.wait_ge(z_lo_ready, 2 * (i - 1))
                for j in range(ND):
                    if i == 0:
                        pe.wait_ge(wp_ready, j + 1)
                    g, c = j // CPG, j % CPG
                    last = pe.matmul(bank[2 * (i % 2) + g // 2][:, (g % 2) * GC:(g % 2 + 1) * GC],
                                     xT[:, i, j, :], wp[:, j, :], start=(c == 0), stop=(c == CPG - 1))
                last.then_inc(z_psum, 1)

            def pool_tokens(i):
                pe.wait_ge(z_hi_ready, 2 * i + 2)
                pe.wait_ge(z_lo_ready, 2 * i + 2)
                if i == 0:
                    pe.wait_ge(band_lo_ready, 1)
                else:
                    pe.wait_ge(h_ready, i)
                for g in range(len(WINDOWS)):
                    dst = bank[4 + g // 2][:, (g % 2) * GC:(g % 2 + 1) * GC]
                    cols = slice(g * GC, (g + 1) * GC)
                    if i == 0:
                        products = [(BAND_FIRST, z_hi, 0), (BAND_FIRST, z_lo, 0)]
                    else:
                        products = [(BAND_NOW, z_hi, i), (BAND_NOW, z_lo, i),
                                    (BAND_PREV, z_hi, i - 1), (BAND_PREV, z_lo, i - 1)]
                    for n, (band, src, tile) in enumerate(products):
                        last = pe.matmul(dst, band_hi[:, band + g, :], src[:, tile, cols],
                                         start=(n == 0), stop=(i > 0 and n == len(products) - 1))
                    if i == 0:
                        last = pe.matmul(dst, band_lo[:, g, :], z_hi[:, 0, cols], start=False, stop=True)
                last.then_inc(mix_done, 1)

            def transpose_h(i):
                pe.wait_ge(h_ready, i + 1)
                if i:
                    pe.wait_ge(hT_ready, 2 * i)
                for b in range(2):
                    for j in range(4):
                        last = pe.transpose(bank[6 + b][:, j * P:(j + 1) * P],
                                            h[:, i, (4 * b + j) * P:(4 * b + j + 1) * P], ident)
                    last.then_inc(hT_psum, 1)

            def logits(i):
                pe.wait_ge(hT_ready, 2 * i + 2)
                for j in range(ND):
                    last = pe.matmul(bank[0][:, i * NR:(i + 1) * NR], hT[:, i, j, :], wr[:, j, :],
                                     start=(j == 0), stop=(j == ND - 1))
                return last

            project(0)
            project(1)
            pool_tokens(0)
            project(2)
            pool_tokens(1)
            pe.wait_ge(consts_loaded, 16)
            transpose_h(0)
            project(3)
            pool_tokens(2)
            transpose_h(1)
            pe.wait_ge(wr_ready, 1)
            logits(0)
            pool_tokens(3)
            transpose_h(2)
            logits(1)
            transpose_h(3)
            logits(2)
            logits(3).then_inc(logits_done, 1)
            pe.wait_ge(mask_ready, 1)
            pe.wait_ge(count_by_ready, 1)
            pe.matmul(bank[1][:, 0:(NT + 1) * E], count_by[:, 0, :], mask[:, :, :], start=True, stop=False)
            for n in range(NT):
                last = pe.matmul(bank[1][:, (n + 1) * E:(NT + 1) * E], count_by[:, 1, :],
                                 mask[:, n:n + 1, :].to_broadcast([P, NT - n, E]), start=False, stop=(n == NT - 1))
            last.then_inc(pos_done, 1)

            def slot_sums(dst, hot, values):
                for i in range(NT):
                    last = pe.matmul(dst, hot[:, i, :], values(i), start=(i == 0), stop=(i == NT - 1))
                return last

            def slot_sums_of(e):
                slot_sums(bank[7][:, 2 * e:2 * e + 2], onehot[:, e], lambda i: value[:, i, e, :]).then_inc(slot_psum, 1)

            for e in range(DVE_HOTS):
                pe.wait_ge(onehot_ready, e + 1)
                slot_sums_of(e)

            def rows_transposed(done):
                for b in range(2):
                    for j in range(4):
                        n = 4 * b + j
                        last = pe.transpose(bank[2 + b][:, j * P:(j + 1) * P], gx[:, n * P:(n + 1) * P], ident)
                    if done:
                        last.then_inc(done, 1)
                return last

            def act_transposed():
                for j in range(NF):
                    last = pe.transpose(bank[4][:, j * P:(j + 1) * P], act[:, j * P:(j + 1) * P], ident)
                return last

            def multiply_chunk(n, c, tiles, high, low):
                pe.wait_ge(hi_ready, n + (c + 1))
                for dst, k, cols, start, _ in tiles:
                    pe.matmul(dst, high[:, k, :], w_hi[:, c, cols], start=start, stop=False)
                    pe.matmul(dst, low[:, k, :], w_hi[:, c, cols], start=False, stop=False)
                pe.wait_ge(lo_ready, n + (c + 1))
                for dst, k, cols, _, stop in tiles:
                    last = pe.matmul(dst, high[:, k, :], w_lo[:, c, cols], start=False, stop=stop)
                last.then_inc(used, 1)

            def up_or_gate(m, n):
                for c in range(CHUNKS):
                    multiply_chunk(n, c, [(bank[m][:, :], 2 * c + a, slice(a * F, (a + 1) * F),
                                           c + a == 0, (c, a) == (CHUNKS - 1, 1)) for a in range(2)], x_hi, x_lo)

            def down(n, first_bank=5):
                for c in range(CHUNKS):
                    multiply_chunk(n, c, [(bank[first_bank + b][:, :], c, slice(b * HALF, (b + 1) * HALF),
                                           c == 0, c == CHUNKS - 1) for b in range(2)], act_hi, act_lo)

            def step(e, first=False, last=False, more_slots=()):
                n = 0 if first else chunks_before(e)
                pe.wait_ge(x_hi_ready, e * 2 + 2)
                pe.wait_ge(x_lo_ready, e * 2 + 2)
                up_or_gate(GATE, n)
                up_or_gate(UP, n + CHUNKS)
                if not last:
                    pe.wait_ge(gx_loaded, e * 16 + 32)
                    rows_transposed(xT_psum)
                for k in more_slots:
                    pe.wait_ge(pool_onehot_ready, k - DVE_HOTS + 1)
                    slot_sums_of(k)
                if not first:
                    pe.wait_ge(act_hi_ready, e)
                    pe.wait_ge(act_lo_ready, e)
                    down(n + 2 * CHUNKS)
                pe.wait_ge(act_ready, e + 1)
                act_transposed().then_inc(actT_psum, 1)

            pe.wait_ge(gx_loaded, 16)
            rows_transposed(xT_psum)
            step(0, first=True, more_slots=range(DVE_HOTS, STEP0_HOTS))
            step(1, more_slots=range(STEP0_HOTS, E))
            with pe.Fori(1, E // 2 - 1) as it:
                step(it * 2)
                step(it * 2 + 1)
            step(E - 2)
            step(E - 1, last=True)
            pe.wait_ge(act_hi_ready, E)
            pe.wait_ge(act_lo_ready, E)
            down(chunks_before(E), LAST_BANK)

            pe.wait_ge(over_ready, 1)
            n_over = pe.value_load(over[0:1, 0:1], min_val=0, max_val=T)
            with pe.If(n_over > 0):
                pe.wait_ge(o_plan, 1)
                for j in range(OV):
                    pe.wait_ge(o_dve, 3 * j + 1)
                    slot_sums(bank[7][:, 0:2], onehot[:, 0], lambda i: ovalue[:, i, j, :]).then_inc(o_pe, 1)
                    pe.wait_ge(o_gx_loaded, 16 * j + 16)
                    rows_transposed(None).then_inc(o_pe, 1)
                    pe.wait_ge(o_dve, 3 * j + 2)
                    pe.wait_ge(o_w_loaded, 48 * j + 48)
                    for m in (GATE, UP):
                        for k in range(ND):
                            last = pe.matmul(bank[m][:, :], oxT[:, k, :], raw_at(0, m)[:, k, :],
                                             start=(k == 0), stop=(k == ND - 1))
                    last.then_inc(o_pe, 1)
                    pe.wait_ge(o_dve, 3 * j + 3)
                    act_transposed().then_inc(o_pe, 1)
                    pe.wait_ge(o_act, 4 * j + 2)
                    for b in range(2):
                        for k in range(NF):
                            last = pe.matmul(bank[5 + b][:, :], oactT[:, k, :],
                                             raw_at(0, DOWN)[:, k, b * HALF:(b + 1) * HALF],
                                             start=(k == 0), stop=(k == NF - 1))
                    last.then_inc(o_pe, 1)
            pe.nop()


_NAMES = ["x", "x_t", "mix_norm", "pool_w", "pool_scale", "ffn_norm", "ffn_norm_t", "w_group_router", "b_group_router",
          "w_expert_router", "b_expert_router", "w_gate", "w_up", "w_down", "final_norm"]


def kernel(**inputs):
    import concourse.bacc as bacc
    from concourse.bass_utils import run_bass_kernel_spmd

    arrays = {}
    for name in _NAMES:
        a = np.ascontiguousarray(inputs[name.removesuffix("_t")])
        arrays[name] = a if name == "final_norm" else a.reshape(a.shape[1:])
    x = arrays["x"]
    arrays["x_t"] = np.ascontiguousarray(x.reshape(x.shape[0] // P, P, -1, P).transpose(3, 0, 2, 1))
    for name in ("mix_norm", "ffn_norm_t"):
        arrays[name] = np.ascontiguousarray(arrays[name].reshape(-1, P).T)
    E, T = arrays["w_gate"].shape[0], arrays["x"].shape[0]
    arrays["bands"], arrays["consts"] = shape_constants(E, T)
    nc = bacc.Bacc("TRN2", target_bir_lowering=False, num_devices=1)
    maps, aps = {}, []
    for name, a in arrays.items():
        maps[f"in_{name}"] = a
        aps.append(nc.dram_tensor(f"in_{name}", a.shape, mybir.dt.from_np(a.dtype), kind="ExternalInput").ap())
    aps.append(nc.dram_tensor("out", arrays["x"].shape, F32, kind="ExternalOutput").ap())
    build(nc, *aps)
    r = run_bass_kernel_spmd(nc, [maps], core_ids=[0])
    return r.results[0]["out"].reshape(inputs["x"].shape)
```

```python
from contextlib import ExitStack

import numpy as np

import concourse.bass as bass
from concourse import mybir

F32 = mybir.dt.float32
F32R = mybir.dt.float32r
F16 = mybir.dt.float16
I32 = mybir.dt.int32
ALU = mybir.AluOpType
ACT = mybir.ActivationFunctionType
AX = mybir.AxisListType

P = 128
EPS = 1e-6
WINDOWS = (2, 4, 8, 16)
TOP_K = 2
FAR = 1e30

FAR_ROW = 2048

BAND_NOW, BAND_PREV, BAND_FIRST, BANDS = 0, 4, 8, 12
IDENT, BEFORE, ONES, SLOT = 0, 1, 2, 3
VEC = 4 * P
DESC, TILE_NO, PAIR, TOKEN = VEC, VEC + 16, VEC + 24, VEC + 28
CONSTS = VEC + 32


def shape_constants(E, T):
    bands = np.zeros((P, BANDS, P), np.float32)
    s, t = np.arange(P)[:, None], np.arange(P)[None, :]
    for g, w in enumerate(WINDOWS):
        eye = (s == t).astype(np.float32)
        now = ((s <= t) & (s > t - w)).astype(np.float32)
        bands[:, BAND_NOW + g] = now / np.float32(w) - eye
        bands[:, BAND_PREV + g] = (s - P > t - w) / np.float32(w)
        bands[:, BAND_FIRST + g] = now / np.minimum(t + 1, w).astype(np.float32) - eye
    c = np.zeros((P, CONSTS), np.float32)
    for n, block in ((IDENT, s == t), (BEFORE, s < t), (ONES, s >= 0), (SLOT, t)):
        c[:, n * P:(n + 1) * P] = block
    c[:, DESC:DESC + E] = E - np.arange(E)
    c[:, TILE_NO:TILE_NO + 8] = np.arange(8)
    for i in range(T // P):
        c[:, PAIR + i] = TOP_K * (i * P + np.arange(P)) - FAR_ROW
        c[:, TOKEN + i] = i * P + np.arange(P) - FAR_ROW
    return bands.reshape(P, BANDS * P), c


def build(nc, x, x_t, router, pool_w, pool_scale, ffn_norm, w_gate, w_up, w_down, final_norm, bands, consts,
          out, G):
    T, D = x.shape
    E, _, F = w_gate.shape
    EPG = E // G
    NT, ND, NF = T // P, D // P, F // P
    GC = D // len(WINDOWS)
    CPG = GC // P
    HALF = D // 2
    NR = G + E
    W = ND * F
    CHUNKS = 4
    C = W // CHUNKS
    BUFS = 4
    STEP = 3 * CHUNKS
    OV = TOP_K * T // P - 1
    SPARE_BANK = 2
    DVE_PARTS = 2
    DVE_HOTS = 6
    STEP0_HOTS = 12
    assert E % 2 == 0 and NF * D == W and HALF == 512 and F == 512 and CPG == 2 and C == 2 * F == D
    assert TOP_K * T <= FAR_ROW // 2 and BUFS == CHUNKS

    rows_dram = nc.dram_tensor("normed_rows", (T, D), F32, kind="Internal").ap()
    parts = nc.dram_tensor("expert_parts", (TOP_K * T, D), F32, kind="Internal").ap()

    with ExitStack() as ctx:
        def sb(name, shape, dt=F32):
            return ctx.enter_context(nc.sbuf_tensor(name, shape, dt))

        def sem(name):
            return ctx.enter_context(nc.semaphore(name))

        bank = [ctx.enter_context(nc.psum_tensor(f"bank{i}", [P, 512], F32)) for i in range(8)]

        raw = sb("raw", [P, 2, 3, W])
        w_hi = sb("w_hi", [P, BUFS, C], F32R)
        w_lo = sb("w_lo", [P, BUFS, C], F32R)
        h = sb("h", [P, NT, D])
        gx = sb("gx", [P, 2, D])
        x_hi = sb("x_hi", [P, ND, P], F32R)
        x_lo = sb("x_lo", [P, ND, P], F32R)
        sil = sb("sil", [P, F])
        act = sb("act", [P, F])
        act_hi = sb("act_hi", [P, NF, P], F32R)
        act_lo = sb("act_lo", [P, NF, P], F32R)
        yrow = sb("yrow", [P, 2, D])
        cst = sb("cst", [P, CONSTS])
        count_by = sb("count_by", [P, 2, P], F16)
        small = sb("small", [P, 2 * ND + NR + ND * NR])
        ss = sb("ss", [P, 3, NT])
        table_in = sb("table_in", [P, 1])
        table_out = sb("table_out", [P, 3])
        ms, inv, root, newton, rstd = (sb(n, [P, 3, NT]) for n in ("ms", "inv", "root", "newton", "rstd"))
        L = sb("L", [P, NT, NR])
        gtmp = sb("gtmp", [P, 4, NT, G])
        gcol = sb("gcol", [P, 10, NT])
        em = sb("em", [P, 2, NT, E])
        etmp = sb("etmp", [P, 2, NT, E])
        oh = sb("oh", [P, TOP_K, NT, E])
        mask = sb("mask", [P, NT + 1, E], F16)
        pos = sb("pos", [P, 2, NT, E])
        value = sb("value", [P, NT, E, 2], F16)
        onehot = sb("onehot", [P, E, NT, P], F16)
        slots = sb("slots", [P, E, 2], I32)
        oslots = sb("oslots", [P, 2], I32)
        wk = sb("wk", [P, TOP_K, NT])
        w_last = sb("w_last", [P, TOP_K, NT])
        weighted = sb("weighted", [P, NT, P])
        weighted_T = sb("weighted_T", [P, NT, P])
        second_weights = weighted
        cnt = sb("cnt", [P, 4, E])
        cmax = sb("cmax", [P, 2])
        over = sb("over", [P, 1], I32)
        ovc = sb("ovc", [P, 3, OV, E])
        ovf = sb("ovf", [P, 4, 8])
        opos = sb("opos", [P, 3, NT, OV])
        ovalue = sb("ovalue", [P, NT, OV, 2], F16)
        expert_no = sb("expert_no", [P, 8], I32)

        xT = raw[:, 1, 0, :].rearrange("p (i j t) -> p i j t", i=NT, j=ND)
        wp = raw[:, 1, 1, 0:ND * GC].rearrange("p (j d) -> p j d", j=ND)
        pscale = raw[:, 1, 1, ND * GC:ND * GC + D]
        rows = raw[:, 1, 2, :].rearrange("p (i d) -> p i d", i=NT)
        ffnb = yrow[:, 0, :]
        band_raw = raw[:, 0, 2, 0:BANDS * P].rearrange("p (n t) -> p n t", n=BANDS)
        hT = xT
        z_hi, z_lo = w_hi, w_lo
        band_now_prev, band_first, band_first_lo = x_hi, x_lo[:, 0:4], x_lo[:, 4:8]
        oxT = raw[:, 1, 0, 0:D].rearrange("p (j t) -> p j t", j=ND)
        oactT = raw[:, 1, 0, D:D + F].rearrange("p (j t) -> p j t", j=NF)
        fnorm = raw[:, 0, 2, 0:D]
        part = raw[:, 0, 0:2, :].rearrange("p a (b k d) -> p (a b) k d", b=2, k=TOP_K)

        mixn, ffnn = small[:, 0:ND], small[:, ND:2 * ND]
        bias = small[:, 2 * ND:2 * ND + NR]
        wr = small[:, 2 * ND + NR:].rearrange("p (j n) -> p j n", j=ND)

        def block_of(n):
            return cst[:, n * P:(n + 1) * P]

        ident = block_of(IDENT)

        x_loaded = [sem(f"x_loaded{i}") for i in range(NT)]
        xT_loaded = [sem(f"xT_loaded{i}") for i in range(NT)]
        bands_loaded = sem("bands_loaded")
        pscale_loaded = sem("pscale_loaded")
        ffnb_loaded = sem("ffnb_loaded")
        consts_loaded = sem("consts_loaded")
        pool_w_loaded = [sem(f"pool_w_loaded{a}") for a in range(2)]
        small_loaded = sem("small_loaded")
        fnorm_loaded = sem("fnorm_loaded")
        w_loaded = [[[sem(f"w{m}_loaded{s}_{a}") for a in range(2)] for m in "gud"] for s in range(2)]
        squared = sem("squared")
        dve = sem("dve")
        inv_ready = sem("inv_ready")
        root_ready = sem("root_ready")
        rstd_ready = sem("rstd_ready")
        wp_ready = sem("wp_ready")
        wr_ready = sem("wr_ready")
        count_by_ready = sem("count_by_ready")
        z_psum = sem("z_psum")
        z_hi_ready = sem("z_hi_ready")
        z_lo_ready = sem("z_lo_ready")
        band_hi_ready = sem("band_hi_ready")
        band_lo_ready = sem("band_lo_ready")
        mix_done = sem("mix_done")
        h_ready = sem("h_ready")
        hT_psum = sem("hT_psum")
        hT_ready = sem("hT_ready")
        r_ready = sem("r_ready")
        rows_stored = sem("rows_stored")
        logits_done = sem("logits_done")
        diff_ready = sem("diff_ready")
        exp_ready = sem("exp_ready")
        mask_ready = sem("mask_ready")
        pos_done = sem("pos_done")
        onehot_ready = sem("onehot_ready")
        slot_psum = sem("slot_psum")
        slots_ready = sem("slots_ready")
        over_ready = sem("over_ready")
        pool_onehot_ready = sem("pool_onehot_ready")
        table_in_cleared = sem("table_in_cleared")
        gx_cleared = sem("gx_cleared")
        storing = sem("storing")
        gathering = sem("gathering")
        gx_loaded = [sem(f"gx_loaded{s}") for s in range(2)]
        yrow_free = sem("yrow_free")
        hi_ready = sem("hi_ready")
        lo_ready = sem("lo_ready")
        used = sem("used")
        xT_psum = sem("xT_psum")
        x_hi_ready = sem("x_hi_ready")
        x_lo_ready = sem("x_lo_ready")
        sil_ready = sem("sil_ready")
        act_ready = sem("act_ready")
        actT_psum = sem("actT_psum")
        act_hi_ready = sem("act_hi_ready")
        act_lo_ready = sem("act_lo_ready")
        y_ready = sem("y_ready")
        y_stored = sem("y_stored")
        o_plan = sem("o_plan")
        o_dve_plan = sem("o_dve_plan")
        o_w_loaded = sem("o_w_loaded")
        o_slots_ready = sem("o_slots_ready")
        o_gx_loaded = sem("o_gx_loaded")
        o_pe = sem("o_pe")
        o_act = sem("o_act")
        o_dve = sem("o_dve")
        o_stored = sem("o_stored")
        weighted_ready = sem("weighted_ready")
        weighted_psum = sem("weighted_psum")
        weighted_T_ready = sem("weighted_T_ready")
        zeros_ready = sem("zeros_ready")
        zeros_stored = sem("zeros_stored")
        part_loaded = [sem(f"part_loaded{i}") for i in range(NT)]
        second_weights_ready = sem("second_weights_ready")
        last_psum = sem("last_psum")
        sum_ready = sem("sum_ready")
        pool_steps = sem("pool_steps")
        last_rstd_ready = sem("last_rstd_ready")
        out_ready = sem("out_ready")
        out_stored = sem("out_stored")

        block = ctx.enter_context(nc.Block())

        def chunks_before(e):
            return e * STEP - CHUNKS

        GATE, UP, DOWN = range(3)

        def weights(e, m):
            return (w_gate, w_up, w_down)[m][e].rearrange("(j p) n -> p j n", p=P)

        def raw_at(s, m):
            return raw[:, s, m, :].rearrange("p (j n) -> p j n", j=(ND, ND, NF)[m])

        def raw_chunk(s, m, c):
            return raw[:, s, m, c * C:(c + 1) * C]

        def halves(t):
            return [t[:, 4 * b:4 * b + 4, :] for b in range(2)]

        def bank4(n):
            return bank[n][:, :].rearrange("p (j t) -> p j t", j=4)

        def newton_step(eng, chain, turn, n, cols):
            eng.wait_ge(root_ready, turn)
            chain(eng.tensor_tensor(newton[:, n, cols], root[:, n, cols], root[:, n, cols], ALU.mult))
            chain(eng.tensor_tensor(newton[:, n, cols], newton[:, n, cols], ms[:, n, cols], ALU.mult))
            chain(eng.tensor_scalar(newton[:, n, cols], newton[:, n, cols], -0.5, 1.5, ALU.mult, ALU.add))
            return eng.tensor_tensor(rstd[:, n, cols], newton[:, n, cols], root[:, n, cols], ALU.mult)

        @block.sync
        def _(sp):
            def load_pool_w(a):
                half = slice(a * (ND // 2), (a + 1) * (ND // 2))
                sp.dma_start(wp[:, half, :], pool_w[2 * a:2 * a + 2].rearrange("g (c p) d -> p (g c) d", p=P))\
                    .then_inc(pool_w_loaded[a], 16)

            def load_xT(i):
                sp.dma_start(xT[:, i], x_t[:, i]).then_inc(xT_loaded[i], 16)

            load_pool_w(0)
            load_xT(0)
            load_pool_w(1)
            load_xT(1)
            load_xT(2)
            sp.dma_start(raw[:, 0, 2, 0:BANDS * P], bands).then_inc(bands_loaded, 16)
            load_xT(3)
            sp.dma_start(ffnb, ffn_norm.partition_broadcast(P)).then_inc(ffnb_loaded, 16)

            def load(e, s, m, a):
                k = (ND, ND, NF)[m] // 2
                sp.dma_start(raw_at(s, m)[:, a * k:(a + 1) * k], weights(e, m)[:, a * k:(a + 1) * k])\
                    .then_inc(w_loaded[s][m][a], 16)

            def load_both(e, s, m):
                load(e, s, m, 0)
                load(e, s, m, 1)

            load_both(0, 0, GATE)
            load_both(0, 0, UP)
            sp.wait_ge(band_hi_ready, 1)
            sp.wait_ge(band_lo_ready, 1)
            load_both(0, 0, DOWN)
            sp.wait_ge(r_ready, NT - 1)
            load_both(1, 1, UP)
            sp.wait_ge(logits_done, 1)
            sp.wait_ge(storing, 1)
            load(1, 1, GATE, 0)
            sp.wait_ge(gathering, 1)
            load(1, 1, GATE, 1)
            sp.wait_ge(rows_stored, 16 * NT)
            load_both(1, 1, DOWN)

            def reload(e, s, m, chunks, second_before):
                for a in range(2):
                    sp.wait_ge(lo_ready, chunks + 2 * a + 2)
                    sp.wait_ge(*second_before[a])
                    load(e, s, m, a)

            reload(2, 0, GATE, 0, ((w_loaded[1][DOWN][0], 16), (w_loaded[1][DOWN][1], 16)))
            reload(2, 0, UP, CHUNKS, ((w_loaded[0][GATE][0], 32), (w_loaded[0][GATE][1], 32)))

            def reload_step(e, s, turn, turn_two_before):
                n = e * STEP - (2 * STEP + CHUNKS)
                same = w_loaded[s]
                reload(e, s, GATE, n, ((same[DOWN][0], turn_two_before), (same[DOWN][1], turn_two_before)))
                reload(e, s, UP, n + CHUNKS, ((same[GATE][0], turn), (same[GATE][1], turn)))
                reload(e - 1, 1 - s, DOWN, n + 2 * CHUNKS, ((same[UP][0], turn), (same[UP][1], turn)))

            with sp.Fori(1, E // 2 - 1) as it:
                turns = [sp.to_reg(it * 16 + 16 * n) for n in range(3)]
                reload_step(it * 2 + 1, 1, turns[1], turns[0])
                reload_step(it * 2 + 2, 0, turns[2], turns[1])
            reload(E - 1, 1, GATE, chunks_before(E - 3),
                   ((w_loaded[1][DOWN][0], 8 * E - 16), (w_loaded[1][DOWN][1], 8 * E - 16)))
            reload(E - 2, 0, DOWN, chunks_before(E - 3) + 2 * CHUNKS,
                   ((w_loaded[1][GATE][0], 8 * E), (w_loaded[1][GATE][1], 8 * E)))
            reload(E - 1, 1, UP, chunks_before(E - 3) + CHUNKS,
                   ((w_loaded[0][DOWN][0], 8 * E), (w_loaded[0][DOWN][1], 8 * E)))
            reload(E - 1, 1, DOWN, chunks_before(E - 2) + 2 * CHUNKS,
                   ((w_loaded[1][UP][0], 8 * E), (w_loaded[1][UP][1], 8 * E)))

            sp.wait_ge(over_ready, 1)
            n_over = sp.value_load(over[0:1, 0:1], min_val=0, max_val=T)
            with sp.If(n_over > 0):
                sp.wait_ge(o_plan, 1)
                for j in range(OV):
                    e = sp.value_load(expert_no[0:1, j:j + 1], min_val=0, max_val=E - 1)
                    if j:
                        sp.wait_ge(o_pe, 5 * j)
                    for m in range(3):
                        sp.dma_start(raw_at(0, m), weights(e, m)).then_inc(o_w_loaded, 16)
                sp.wait_ge(o_stored, 16 * OV)
            sp.nop()
            sp.wait_ge(lo_ready, chunks_before(E - 1) + 2 * CHUNKS)
            sp.dma_start(fnorm, final_norm.partition_broadcast(P)).then_inc(fnorm_loaded, 16)
            sp.wait_ge(zeros_stored, 16)
            sp.wait_ge(y_stored, 16 * (E - 1))
            for i in range(NT):
                sp.dma_start(part[:, i], parts[i * TOP_K * P:(i + 1) * TOP_K * P, :]
                             .rearrange("(p k) d -> p k d", k=TOP_K)).then_inc(part_loaded[i], 16)
            for i in range(NT):
                sp.wait_ge(out_ready, i + 1)
                sp.dma_start(out[i * P:(i + 1) * P, :], h[:, i, :]).then_inc(out_stored, 16)
            sp.wait_ge(out_stored, 16 * NT)

        @block.gpsimd
        def _(pool):
            pool.dma_start(small[:, :], router).then_inc(small_loaded, 16)
            pool.memset(table_in[:, :], 0.0).then_inc(table_in_cleared, 1)
            pool.memset(gx[:, :, :], 0.0).then_inc(gx_cleared, 1)
            pool.memset(yrow[:, 1, :], 0.0).then_inc(zeros_ready, 1)
            pool.dma_start(cst[:, :], consts).then_inc(consts_loaded, 16)
            for i in range(NT):
                pool.wait_ge(r_ready, i + 1)
                pool.dma_start(rows_dram[i * P:(i + 1) * P, :], rows[:, i, :]).then_inc(rows_stored, 16)
            pool.sem_inc(storing, 1)
            pool.sem_inc(yrow_free, 1)
            pool.wait_ge(rows_stored, 16 * NT)
            pool.wait_ge(gx_cleared, 1)

            def gather(index, parity, done):
                return pool.indirect_dma_start(gx[:, parity, :], None, rows_dram, bass.IndirectOffsetOnAxis(index, 0),
                                               bounds_check=T - 1, oob_is_err=False).then_inc(done, 16)

            def scatter(index, parity, done):
                pool.indirect_dma_start(parts, bass.IndirectOffsetOnAxis(index, 0), yrow[:, parity, :], None,
                                        bounds_check=TOP_K * T - 1, oob_is_err=False).then_inc(done, 16)

            def store_results(e):
                pool.wait_ge(y_ready, 2 * e + 2)
                scatter(slots[:, e, 0:1], e % 2, y_stored)

            pool.wait_ge(slots_ready, 1)
            gather(slots[:, 0, 1:2], 0, gx_loaded[0])

            def one_hots(experts):
                for e in experts:
                    for i in range(NT):
                        ins = pool.tensor_scalar(onehot[:, e, i, :], block_of(SLOT), pos[:, 1, i, e:e + 1],
                                                 None, ALU.is_equal)
                        if (e, i) == (DVE_HOTS, 0):
                            ins.then_inc(gathering, 1)
                    ins.then_inc(pool_onehot_ready, 1)

            one_hots(range(DVE_HOTS, DVE_HOTS + 1))
            pool.wait_ge(slots_ready, 2)
            gather(slots[:, 1, 1:2], 1, gx_loaded[1])
            one_hots(range(DVE_HOTS + 1, DVE_HOTS + 3))
            pool.wait_ge(xT_psum, 2)
            gather(slots[:, 2, 1:2], 0, gx_loaded[0])
            one_hots(range(DVE_HOTS + 3, E))
            for e in range(E):
                if e < E - 3:
                    pool.wait_ge(xT_psum, 2 * (e + 2))
                    gather(slots[:, e + 3, 1:2], (e + 3) % 2, gx_loaded[(e + 3) % 2])
                if e == 1:
                    pool.wait_ge(slots_ready, 3)
                    pool.wait_ge(zeros_ready, 1)
                    scatter(slots[:, E - 1, 0:1], 1, zeros_stored)
                if e == 2:
                    pool.wait_ge(zeros_stored, 16)
                    pool.sem_inc(yrow_free, 1)
                if e >= 2:
                    pool.wait_ge(y_stored, 16 * (e - 1))
                    pool.sem_inc(yrow_free, 1)
                if e:
                    store_results(e - 1)
            pool.wait_ge(y_stored, 16 * (E - 1))
            pool.sem_inc(yrow_free, 1)

            pool.wait_ge(over_ready, 1)
            n_over = pool.value_load(over[0:1, 0:1], min_val=0, max_val=T)
            with pool.If(n_over > 0):
                for j in range(OV):
                    pool.wait_ge(o_slots_ready, j + 1)
                    gather(oslots[:, 1:2], 0, o_gx_loaded)
                    pool.wait_ge(o_act, 4 * j + 4)
                    scatter(oslots[:, 0:1], 0, o_stored)
            pool.nop()

            def chain(ins):
                ins.then_inc(pool_steps, 1)
                steps[0] += 1
                pool.wait_ge(pool_steps, steps[0])

            steps = [0]
            for i in range(NT):
                pool.wait_ge(inv_ready, 5 + i)
                newton_step(pool, chain, 5 + i, 2, slice(i, i + 1)).then_inc(last_rstd_ready, 1)

        @block.scalar
        def _(actv):
            actv.dma_start(pscale, pool_scale.partition_broadcast(P)).then_inc(pscale_loaded, 16)
            for i in range(NT):
                actv.dma_start(h[:, i, :], x[i * P:(i + 1) * P, :]).then_inc(x_loaded[i], 16)

            def load_table(turn, function):
                actv.activation(table_out[:, turn:turn + 1], table_in[:, :], function)

            actv.wait_ge(table_in_cleared, 1)
            load_table(0, ACT.Sqrt)
            actv.wait_ge(gx_cleared, 1)

            def square(n, i):
                if n + i:
                    actv.wait_ge(squared, n * NT + i)
                actv.activation(gx[:, 0, :], h[:, i, :], ACT.Square, accum_out=ss[:, n, i:i + 1]).then_inc(squared, 1)

            def square_root(turn, n, cols):
                actv.wait_ge(inv_ready, turn)
                actv.activation(root[:, n, cols], inv[:, n, cols], ACT.Sqrt).then_inc(root_ready, 1)

            def norm_z(i):
                actv.wait_ge(z_psum, i + 1)
                for b in range(2):
                    cols = slice(b * HALF, (b + 1) * HALF)
                    actv.activation(z_hi[:, i, cols], bank[2 * i + b][:, :], ACT.Copy,
                                    scale=rstd[:, 0, i:i + 1]).then_inc(z_hi_ready, 1)

            def copy_hT(i):
                for b in range(2):
                    actv.wait_ge(hT_psum, 2 * i + b + 1)
                    actv.activation(hT[:, i, 4 * b:4 * b + 4, :], bank4(4 + b), ACT.Copy).then_inc(hT_ready, 1)

            def square_h(i):
                actv.wait_ge(h_ready, i + 1)
                square(1, i)

            def square_x(i):
                actv.wait_ge(x_loaded[i], 16)
                square(0, i)

            square_x(0)
            square_x(1)
            square_root(1, 0, slice(0, 2))
            square_x(2)
            actv.wait_ge(rstd_ready, 1)
            norm_z(0)
            square_x(3)
            square_root(2, 0, slice(2, 4))
            norm_z(1)
            actv.wait_ge(bands_loaded, 16)
            actv.activation(band_now_prev[:, :, :], band_raw[:, BAND_NOW:BAND_FIRST], ACT.Copy)
            actv.activation(band_first, band_raw[:, BAND_FIRST:BANDS], ACT.Copy).then_inc(band_hi_ready, 1)
            actv.wait_ge(rstd_ready, 2)
            norm_z(2)
            norm_z(3)
            actv.wait_ge(consts_loaded, 16)
            actv.activation(count_by[:, :, :], cst[:, BEFORE * P:(ONES + 1) * P].rearrange("p (n t) -> p n t", n=2),
                            ACT.Copy).then_inc(count_by_ready, 1)
            square_h(0)
            copy_hT(0)
            square_h(1)
            square_root(3, 1, slice(0, 2))
            copy_hT(1)
            square_h(2)
            copy_hT(2)
            square_h(3)
            square_root(4, 1, slice(2, 4))
            copy_hT(3)
            actv.wait_ge(diff_ready, 1)
            actv.activation(gtmp[:, 1], gtmp[:, 0], ACT.Exp).then_inc(exp_ready, 1)
            actv.wait_ge(diff_ready, 2)
            actv.activation(gcol[:, 7], gcol[:, 6], ACT.Exp).then_inc(exp_ready, 1)
            load_table(1, ACT.Silu)
            actv.wait_ge(logits_done, 1)

            def round_chunks(m, s, turn, first_chunk, wait=True, chunks=range(CHUNKS)):
                for c in chunks:
                    if c % 2 == 0:
                        actv.wait_ge(w_loaded[s][m][c // 2], turn)
                    if wait:
                        actv.wait_ge(used, first_chunk + (c + 1 - BUFS))
                    actv.activation(w_hi[:, c, :], raw_chunk(s, m, c), ACT.Copy).then_inc(hi_ready, 1)

            def rows_high(e):
                for b, dst in enumerate(halves(x_hi)):
                    actv.wait_ge(xT_psum, e * 2 + (b + 1))
                    actv.activation(dst, bank4(2 + b), ACT.Copy).then_inc(x_hi_ready, 1)

            def act_high(e):
                actv.wait_ge(actT_psum, e + 1)
                actv.activation(act_hi[:, :, :], bank4(4), ACT.Copy).then_inc(act_hi_ready, 1)

            def results(e, parity, first_bank=5):
                actv.wait_ge(yrow_free, e + 1)
                for b in range(2):
                    actv.activation(yrow[:, parity, b * HALF:(b + 1) * HALF], bank[first_bank + b][:, :], ACT.Copy)\
                        .then_inc(y_ready, 1)

            def step(e, s, turn, turn_before, first=False, second=False):
                n = 0 if first else chunks_before(e)
                if not first:
                    round_chunks(GATE, s, turn, n)
                    if not second:
                        results(e - 2, s)
                    act_high(e - 1)
                round_chunks(UP, s, turn, n + CHUNKS)
                if not first:
                    actv.wait_ge(act_ready, e)
                actv.activation(sil[:, :], bank[0][:, :], ACT.Silu).then_inc(sil_ready, 1)
                if not first:
                    round_chunks(DOWN, 1 - s, turn_before, n + 2 * CHUNKS)
                rows_high(e + 1)

            round_chunks(GATE, 0, 16, 0, wait=False)
            rows_high(0)
            actv.wait_ge(weighted_psum, 1)
            actv.activation(weighted_T[:, :, :], bank4(4), ACT.Copy).then_inc(weighted_T_ready, 1)
            step(0, 0, 16, None, first=True)
            step(1, 1, 16, 16, second=True)
            with actv.Fori(1, E // 2 - 1) as it:
                step(it * 2, 0, it * 16 + 16, it * 16)
                step(it * 2 + 1, 1, it * 16 + 16, it * 16 + 16)
            step(E - 2, 0, 8 * E, 8 * E - 16)
            n = chunks_before(E - 1)
            round_chunks(GATE, 1, 8 * E, n)
            act_high(E - 2)
            results(E - 3, 1)
            round_chunks(DOWN, 0, 8 * E, n + CHUNKS)
            actv.wait_ge(act_ready, E - 1)
            actv.activation(sil[:, :], bank[0][:, :], ACT.Silu).then_inc(sil_ready, 1)
            round_chunks(UP, 1, 8 * E, n + 2 * CHUNKS, chunks=range(CHUNKS // 2))
            actv.wait_ge(used, n + 2 * CHUNKS)
            results(E - 2, 0, SPARE_BANK)
            round_chunks(UP, 1, 8 * E, n + 2 * CHUNKS, chunks=range(CHUNKS // 2, CHUNKS))
            act_high(E - 1)
            round_chunks(DOWN, 1, 8 * E, chunks_before(E))
            actv.wait_ge(used, chunks_before(E) + CHUNKS)
            results(E - 1, 1)

            actv.wait_ge(over_ready, 1)
            n_over = actv.value_load(over[0:1, 0:1], min_val=0, max_val=T)
            with actv.If(n_over > 0):
                actv.wait_ge(yrow_free, E + 1)
                with actv.Fori(0, OV) as j:
                    actv.wait_ge(o_pe, j * 5 + 3)
                    actv.activation(sil[:, :], bank[0][:, :], ACT.Silu).then_inc(o_act, 1)
                    actv.wait_ge(o_pe, j * 5 + 4)
                    actv.activation(oactT, bank4(4), ACT.Copy).then_inc(o_act, 1)
                    actv.wait_ge(o_pe, j * 5 + 5)
                    for b in range(2):
                        actv.activation(yrow[:, 0, b * HALF:(b + 1) * HALF], bank[5 + b][:, :], ACT.Copy)\
                            .then_inc(o_act, 1)
            actv.nop()
            load_table(2, ACT.Sqrt)
            for i in range(NT):
                actv.wait_ge(sum_ready, i + 1)
                square(2, i)
                if i:
                    for t in range(0 if i == 1 else i, i + 1):
                        square_root(5 + t, 2, slice(t, t + 1))

        @block.vector
        def _(v):
            steps = {"dve": 0, "o_dve_plan": 0}

            def chain(ins, own="dve"):
                done = dve if own == "dve" else o_dve_plan
                steps[own] += 1
                ins.then_inc(done, 1)
                v.wait_ge(done, steps[own])

            def inverse_mean(n, cols):
                v.wait_ge(squared, n * NT + cols.stop)
                chain(v.tensor_scalar(ms[:, n, cols], ss[:, n, cols], 1.0 / D, EPS, ALU.mult, ALU.add))
                v.reciprocal(inv[:, n, cols], ms[:, n, cols]).then_inc(inv_ready, 1)

            def rsqrt_mean(turn, n, cols):
                inverse_mean(n, cols)
                return newton_step(v, chain, turn, n, cols)

            def rest(dst, src, high):
                return v.tensor_tensor(dst, src, high.bitcast(F32), ALU.subtract)

            v.wait_ge(small_loaded, 16)
            v.wait_ge(pscale_loaded, 16)
            for j in range(ND):
                if j % (ND // 2) == 0:
                    v.wait_ge(pool_w_loaded[j // (ND // 2)], 16)
                g = j // CPG
                v.scalar_tensor_tensor(wp[:, j, :], wp[:, j, :], mixn[:, j:j + 1], pscale[:, g * GC:(g + 1) * GC],
                                       ALU.mult, ALU.mult).then_inc(wp_ready, 1)

            def z_low(i):
                for b in range(2):
                    v.wait_ge(z_hi_ready, 2 * i + b + 1)
                    cols = slice(b * HALF, (b + 1) * HALF)
                    v.scalar_tensor_tensor(z_lo[:, i, cols], bank[2 * i + b][:, :], rstd[:, 0, i:i + 1],
                                           z_hi[:, i, cols].bitcast(F32), ALU.mult, ALU.subtract)\
                        .then_inc(z_lo_ready, 1)

            def add_mixed(i):
                v.wait_ge(mix_done, i + 1)
                for b in range(2):
                    cols = slice(b * HALF, (b + 1) * HALF)
                    ins = v.tensor_tensor(h[:, i, cols], bank[2 * (i % 2) + b][:, :], h[:, i, cols], ALU.add)
                ins.then_inc(h_ready, 1)

            def norm_rows(i):
                v.scalar_tensor_tensor(rows[:, i, :], h[:, i, :], rstd[:, 1, i:i + 1], ffnb, ALU.mult, ALU.mult)\
                    .then_inc(r_ready, 1)

            rsqrt_mean(1, 0, slice(0, 2)).then_inc(rstd_ready, 1)
            v.wait_ge(rstd_ready, 1)
            z_low(0)
            rsqrt_mean(2, 0, slice(2, 4)).then_inc(rstd_ready, 1)
            v.wait_ge(rstd_ready, 2)
            z_low(1)
            v.wait_ge(band_hi_ready, 1)
            rest(band_first_lo, band_raw[:, BAND_FIRST:BANDS], band_first).then_inc(band_lo_ready, 1)
            z_low(2)
            z_low(3)
            v.tensor_tensor(wr, wr, ffnn.unsqueeze(2).to_broadcast([P, ND, NR]), ALU.mult).then_inc(wr_ready, 1)
            v.memset(mask[:, NT, :], 0.0)
            add_mixed(0)
            add_mixed(1)
            v.wait_ge(ffnb_loaded, 16)
            chain(rsqrt_mean(3, 1, slice(0, 2)))
            add_mixed(2)
            norm_rows(0)
            norm_rows(1)
            add_mixed(3)
            chain(rsqrt_mean(4, 1, slice(2, 4)))
            norm_rows(2)
            norm_rows(3)

            v.wait_ge(logits_done, 1)
            chain(v.tensor_tensor(L[:, :, :], bank[6][:, 0:NT * NR].rearrange("p (i n) -> p i n", i=NT),
                                  rstd[:, 1, :].unsqueeze(2).to_broadcast([P, NT, NR]), ALU.mult))
            chain(v.tensor_tensor(L[:, :, :], L[:, :, :], bias.unsqueeze(1).to_broadcast([P, NT, NR]), ALU.add))
            gl, el = L[:, :, 0:G], L[:, :, G:NR]

            def wide(col, n):
                return col.unsqueeze(2).to_broadcast([P, NT, n])

            def first_largest(vals, n, top, tmp, one_hot, rank):
                chain(v.tensor_tensor(tmp, vals, wide(top, n), ALU.is_equal))
                chain(v.tensor_tensor(tmp, tmp, cst[:, DESC + E - n:DESC + E].unsqueeze(1)
                                      .to_broadcast([P, NT, n]), ALU.mult))
                chain(v.tensor_reduce(rank, tmp, AX.X, ALU.max))
                chain(v.tensor_tensor(one_hot, tmp, wide(rank, n), ALU.is_equal))

            chain(v.tensor_reduce(gcol[:, 0], gl, AX.X, ALU.max))
            v.tensor_tensor(gtmp[:, 0], gl, wide(gcol[:, 0], G), ALU.subtract).then_inc(diff_ready, 1)
            first_largest(gl, G, gcol[:, 0], gtmp[:, 2], gtmp[:, 3], gcol[:, 1])
            chain(v.tensor_scalar(gtmp[:, 2], gtmp[:, 3], FAR, -FAR, ALU.mult, ALU.add))
            for i in range(NT):
                ins = v.tensor_tensor(em[:, 0, i].rearrange("p (g e) -> p g e", g=G),
                                      el[:, i].rearrange("p (g e) -> p g e", g=G),
                                      gtmp[:, 2, i].unsqueeze(2).to_broadcast([P, G, EPG]), ALU.add)
            chain(ins)
            chain(v.tensor_reduce(gcol[:, 2], em[:, 0], AX.X, ALU.max))
            first_largest(em[:, 0], E, gcol[:, 2], etmp[:, 0], oh[:, 0], gcol[:, 3])
            chain(v.scalar_tensor_tensor(em[:, 1], oh[:, 0], -3 * FAR, em[:, 0], ALU.mult, ALU.add))
            chain(v.tensor_reduce(gcol[:, 4], em[:, 1], AX.X, ALU.max))
            first_largest(em[:, 1], E, gcol[:, 4], etmp[:, 1], oh[:, 1], gcol[:, 5])
            v.tensor_tensor(mask[:, 0:NT, :], oh[:, 0], oh[:, 1], ALU.add).then_inc(mask_ready, 1)
            v.tensor_tensor(gcol[:, 6], gcol[:, 4], gcol[:, 2], ALU.subtract).then_inc(diff_ready, 1)
            v.tensor_tensor(value[:, :, :, 0], oh[:, 1], wide(cst[:, PAIR:PAIR + NT], E), ALU.add)
            chain(v.tensor_copy(value[:, :, :, 1], wide(cst[:, TOKEN:TOKEN + NT], E)))

            v.wait_ge(pos_done, 1)
            chain(v.scalar_tensor_tensor(pos[:, 0], bank[1][:, 0:NT * E].rearrange("p (i e) -> p i e", i=NT), 1.0,
                                         mask[:, 0:NT, :], ALU.add, ALU.mult))
            chain(v.tensor_scalar(pos[:, 1], pos[:, 0], -1.0, None, ALU.add))

            def one_hots(experts):
                for e in experts:
                    for i in range(NT):
                        ins = v.tensor_scalar(onehot[:, e, i, :], block_of(SLOT), pos[:, 1, i, e:e + 1], None,
                                              ALU.is_equal)
                    ins.then_inc(onehot_ready, 1)

            one_hots(range(2))

            def slot_numbers(dst, src):
                return v.tensor_scalar(dst, src, float(FAR_ROW), None, ALU.add)

            slot_bank = bank[7][:, 0:2 * E].rearrange("p (e w) -> p e w", w=2)
            v.wait_ge(slot_psum, 1)
            slot_numbers(slots[:, 0, :], bank[6][:, 0:2]).then_inc(slots_ready, 1)
            v.tensor_copy(cnt[:, 0], bank[1][:, NT * E:NT * E + E])
            one_hots(range(2, DVE_HOTS))

            v.wait_ge(exp_ready, 2)
            chain(v.tensor_reduce(gcol[:, 8], gtmp[:, 1], AX.X, ALU.add))
            chain(v.scalar_tensor_tensor(gcol[:, 9], gcol[:, 7], 1.0, gcol[:, 8], ALU.add, ALU.mult))
            chain(v.reciprocal(wk[:, 0], gcol[:, 9]))
            chain(v.tensor_tensor(wk[:, 1], wk[:, 0], gcol[:, 7], ALU.mult))
            for k in range(TOP_K):
                ins = v.tensor_tensor(w_last[:, k], oh[:, k, :, E - 1], wk[:, k], ALU.mult)
            chain(ins)
            chain(v.tensor_tensor(w_last[:, 0], w_last[:, 0], w_last[:, 1], ALU.add))
            for i in range(NT):
                ins = v.tensor_scalar(weighted[:, i, :], block_of(SLOT), pos[:, 1, i, E - 1:E],
                                      w_last[:, 0, i:i + 1], ALU.is_equal, ALU.mult)
            ins.then_inc(weighted_ready, 1)
            chain(v.tensor_reduce(cmax[:, 0:1], cnt[:, 0], AX.X, ALU.max))
            chain(v.tensor_scalar(cmax[:, 1:2], cmax[:, 0:1], -float(P), 0.0, ALU.add, ALU.max))
            v.tensor_copy(over[:, :], cmax[:, 1:2]).then_inc(over_ready, 1)
            v.wait_ge(slot_psum, DVE_HOTS)
            slot_numbers(slots[:, 1:DVE_HOTS, :], slot_bank[:, 1:DVE_HOTS, :]).then_inc(slots_ready, 1)

            def rests_of_chunks(m, s, first_chunk, chunks=range(CHUNKS)):
                for c in chunks:
                    v.wait_ge(hi_ready, first_chunk + (c + 1))
                    rest(w_lo[:, c, :], raw_chunk(s, m, c), w_hi[:, c, :]).then_inc(lo_ready, 1)

            def rows_low(e):
                for b, (dst, high) in enumerate(zip(halves(x_lo), halves(x_hi))):
                    v.wait_ge(x_hi_ready, e * 2 + (b + 1))
                    rest(dst, bank4(2 + b), high).then_inc(x_lo_ready, 1)

            def act_low(e):
                v.wait_ge(act_hi_ready, e + 1)
                rest(act_lo[:, :, :], bank4(4), act_hi[:, :, :]).then_inc(act_lo_ready, 1)

            def step(e, s, first=False, second=False):
                n = 0 if first else chunks_before(e)
                if not first:
                    rests_of_chunks(GATE, s, n)
                    act_low(e - 1)
                rests_of_chunks(UP, s, n + CHUNKS)
                if not first:
                    rests_of_chunks(DOWN, 1 - s, n + 2 * CHUNKS, range(CHUNKS - 1))
                v.wait_ge(sil_ready, e + 1)
                v.wait_ge(used, n + 2 * CHUNKS)
                v.tensor_tensor(act[:, :], sil[:, :], bank[1][:, :], ALU.mult).then_inc(act_ready, 1)
                if not first:
                    rests_of_chunks(DOWN, 1 - s, n + 2 * CHUNKS, range(CHUNKS - 1, CHUNKS))
                rows_low(e + 1)
                if second:
                    v.wait_ge(slot_psum, E)
                    slot_numbers(slots[:, DVE_HOTS:E, :], slot_bank[:, DVE_HOTS:E, :]).then_inc(slots_ready, 1)

            rests_of_chunks(GATE, 0, 0, range(CHUNKS // 2))
            rows_low(0)
            rests_of_chunks(GATE, 0, 0, range(CHUNKS // 2, CHUNKS))
            step(0, 0, first=True)
            step(1, 1, second=True)
            with v.Fori(1, E // 2 - 1) as it:
                step(it * 2, 0)
                step(it * 2 + 1, 1)
            step(E - 2, 0)
            n = chunks_before(E - 1)
            rests_of_chunks(GATE, 1, n)
            act_low(E - 2)
            rests_of_chunks(DOWN, 0, n + CHUNKS)
            rests_of_chunks(UP, 1, n + 2 * CHUNKS)
            for i in range(NT):
                ins = v.tensor_scalar(second_weights[:, i, :], ident, wk[:, 1, i:i + 1], None, ALU.mult)
            ins.then_inc(second_weights_ready, 1)
            v.wait_ge(sil_ready, E)
            v.wait_ge(used, n + 3 * CHUNKS)
            v.tensor_tensor(act[:, :], sil[:, :], bank[1][:, :], ALU.mult).then_inc(act_ready, 1)
            act_low(E - 1)
            rests_of_chunks(DOWN, 1, chunks_before(E))

            n_over = v.value_load(over[0:1, 0:1], min_val=0, max_val=T)
            with v.If(n_over > 0):
                def plan(ins):
                    chain(ins, "o_dve_plan")

                plan(v.memset(cnt[:, 1], 0.0))
                for n in range(1, NT):
                    plan(v.scalar_tensor_tensor(cnt[:, 1], cnt[:, 0], float(n * P), cnt[:, 1], ALU.is_gt, ALU.add))
                src = 1
                for n in range(4):
                    dst = 2 + n % 2
                    d = 1 << n
                    v.tensor_copy(cnt[:, dst, 0:d], cnt[:, src, 0:d])
                    plan(v.tensor_tensor(cnt[:, dst, d:E], cnt[:, src, d:E], cnt[:, src, 0:E - d], ALU.add))
                    src = dst
                over_all = [P, OV, E]
                passed, mine = ovc[:, 0], ovc[:, 2]
                plan(v.tensor_tensor(passed, cnt[:, src].unsqueeze(1).to_broadcast(over_all),
                                      cst[:, TILE_NO:TILE_NO + OV].unsqueeze(2).to_broadcast(over_all), ALU.is_le))
                plan(v.tensor_reduce(ovf[:, 0, 0:OV], passed, AX.X, ALU.add))
                plan(v.tensor_tensor(ovc[:, 1], passed, cnt[:, 1].unsqueeze(1).to_broadcast(over_all), ALU.mult))
                plan(v.tensor_reduce(ovf[:, 1, 0:OV], ovc[:, 1], AX.X, ALU.add))
                plan(v.tensor_tensor(ovf[:, 2, 0:OV], cst[:, TILE_NO:TILE_NO + OV], ovf[:, 1, 0:OV], ALU.subtract))
                plan(v.tensor_scalar(ovf[:, 3, 0:OV], ovf[:, 2, 0:OV], 1.0, float(P), ALU.add, ALU.mult))
                v.tensor_scalar(mine[:, :, 0:1], passed[:, :, 0:1], -1.0, 1.0, ALU.mult, ALU.add)
                plan(v.tensor_tensor(mine[:, :, 1:E], passed[:, :, 0:E - 1], passed[:, :, 1:E], ALU.subtract))
                for i in range(NT):
                    plan(v.tensor_tensor(ovc[:, 1], mine, pos[:, 1, i].unsqueeze(1).to_broadcast(over_all), ALU.mult))
                    plan(v.tensor_reduce(opos[:, 0, i], ovc[:, 1], AX.X, ALU.add))
                    plan(v.tensor_tensor(opos[:, 1, i], opos[:, 0, i], ovf[:, 3, 0:OV], ALU.subtract))
                    plan(v.tensor_tensor(ovc[:, 1], mine, oh[:, 1, i].unsqueeze(1).to_broadcast(over_all), ALU.mult))
                    plan(v.tensor_reduce(opos[:, 2, i], ovc[:, 1], AX.X, ALU.add))
                    v.tensor_scalar(ovalue[:, i, :, 0], opos[:, 2, i], cst[:, PAIR + i:PAIR + i + 1], None, ALU.add)
                    plan(v.tensor_copy(ovalue[:, i, :, 1], cst[:, TOKEN + i:TOKEN + i + 1].to_broadcast([P, OV])))
                plan(v.tensor_scalar(ovf[:, 1, 0:OV], ovf[:, 0, 0:OV], float(E - 1), None, ALU.min))
                v.wait_ge(yrow_free, E + 1)
                v.tensor_copy(expert_no[:, 0:OV], ovf[:, 1, 0:OV]).then_inc(o_plan, 1)
                for j in range(OV):
                    if j:
                        v.wait_ge(o_stored, 16 * j)
                    for i in range(NT):
                        ins = v.tensor_scalar(onehot[:, 0, i, :], block_of(SLOT), opos[:, 1, i, j:j + 1], None,
                                              ALU.is_equal)
                    ins.then_inc(o_dve, 1)
                    v.wait_ge(o_pe, 5 * j + 1)
                    slot_numbers(oslots[:, :], bank[7][:, 0:2]).then_inc(o_slots_ready, 1)
                    v.wait_ge(o_pe, 5 * j + 2)
                    v.tensor_copy(halves(oxT)[0], bank4(2))
                    v.tensor_copy(halves(oxT)[1], bank4(3)).then_inc(o_dve, 1)
                    v.wait_ge(o_act, 4 * j + 1)
                    v.tensor_tensor(act[:, :], sil[:, :], bank[1][:, :], ALU.mult).then_inc(o_dve, 1)
            v.nop()

            v.wait_ge(fnorm_loaded, 16)

            def add_parts(i):
                v.wait_ge(part_loaded[i], 16)
                for k in range(TOP_K if i < DVE_PARTS else 1):
                    chain(v.scalar_tensor_tensor(h[:, i, :], part[:, i, k, :], wk[:, k, i:i + 1], h[:, i, :],
                                                 ALU.mult, ALU.add))

            def add_others(i):
                v.wait_ge(last_psum, i + 1)
                for b in range(2):
                    cols = slice(b * HALF, (b + 1) * HALF)
                    ins = v.tensor_tensor(h[:, i, cols], bank[2 * i + b][:, :], h[:, i, cols], ALU.add)
                ins.then_inc(sum_ready, 1)

            def finish(i):
                v.wait_ge(last_rstd_ready, i + 1)
                v.scalar_tensor_tensor(h[:, i, :], h[:, i, :], rstd[:, 2, i:i + 1], fnorm,
                                       ALU.mult, ALU.mult).then_inc(out_ready, 1)

            add_parts(0)
            add_parts(1)
            add_others(0)
            add_others(1)
            add_parts(2)
            inverse_mean(2, slice(0, 1))
            inverse_mean(2, slice(1, 2))
            add_parts(3)
            add_others(2)
            finish(0)
            inverse_mean(2, slice(2, 3))
            add_others(3)
            finish(1)
            inverse_mean(2, slice(3, 4))
            finish(2)
            finish(3)

        @block.tensor
        def _(pe):
            def project(i):
                pe.wait_ge(xT_loaded[i], 16)
                for j in range(ND):
                    if i == 0:
                        pe.wait_ge(wp_ready, j + 1)
                    g, c = j // CPG, j % CPG
                    last = pe.matmul(bank[2 * i + g // 2][:, (g % 2) * GC:(g % 2 + 1) * GC],
                                     xT[:, i, j, :], wp[:, j, :], start=(c == 0), stop=(c == CPG - 1))
                last.then_inc(z_psum, 1)

            def pool_tokens(i):
                pe.wait_ge(z_hi_ready, 2 * i + 2)
                pe.wait_ge(z_lo_ready, 2 * i + 2)
                if i == 0:
                    pe.wait_ge(band_lo_ready, 1)
                if i >= 2:
                    pe.wait_ge(h_ready, i - 1)
                for g in range(len(WINDOWS)):
                    dst = bank[2 * (i % 2) + g // 2][:, (g % 2) * GC:(g % 2 + 1) * GC]
                    cols = slice(g * GC, (g + 1) * GC)
                    if i == 0:
                        products = [(band_first, z_hi, 0), (band_first, z_lo, 0), (band_first_lo, z_hi, 0)]
                    else:
                        now, prev = band_now_prev[:, 0:4], band_now_prev[:, 4:8]
                        products = [(now, z_hi, i), (now, z_lo, i), (prev, z_hi, i - 1), (prev, z_lo, i - 1)]
                    for n, (band, src, tile) in enumerate(products):
                        last = pe.matmul(dst, band[:, g, :], src[:, tile, cols],
                                         start=(n == 0), stop=(n == len(products) - 1))
                last.then_inc(mix_done, 1)

            def transpose_h(i):
                pe.wait_ge(h_ready, i + 1)
                if i:
                    pe.wait_ge(hT_ready, 2 * i)
                for b in range(2):
                    for j in range(4):
                        last = pe.transpose(bank[4 + b][:, j * P:(j + 1) * P],
                                            h[:, i, (4 * b + j) * P:(4 * b + j + 1) * P], ident)
                    last.then_inc(hT_psum, 1)

            def logits(i):
                pe.wait_ge(hT_ready, 2 * i + 2)
                if i == 0:
                    pe.wait_ge(z_lo_ready, 2 * NT)
                for j in range(ND):
                    last = pe.matmul(bank[6][:, i * NR:(i + 1) * NR], hT[:, i, j, :], wr[:, j, :],
                                     start=(j == 0), stop=(j == ND - 1))
                return last

            for i in range(NT):
                project(i)
            pool_tokens(0)
            pool_tokens(1)
            pe.wait_ge(consts_loaded, 16)
            transpose_h(0)
            pool_tokens(2)
            transpose_h(1)
            pe.wait_ge(wr_ready, 1)
            logits(0)
            pool_tokens(3)
            transpose_h(2)
            logits(1)
            transpose_h(3)
            logits(2)
            logits(3).then_inc(logits_done, 1)
            pe.wait_ge(mask_ready, 1)
            pe.wait_ge(count_by_ready, 1)
            pe.matmul(bank[1][:, 0:(NT + 1) * E], count_by[:, 0, :], mask[:, :, :], start=True, stop=False)
            for n in range(NT):
                last = pe.matmul(bank[1][:, (n + 1) * E:(NT + 1) * E], count_by[:, 1, :],
                                 mask[:, n:n + 1, :].to_broadcast([P, NT - n, E]), start=False, stop=(n == NT - 1))
            last.then_inc(pos_done, 1)

            def slot_sums(dst, hot, values):
                for i in range(NT):
                    last = pe.matmul(dst, hot[:, i, :], values(i), start=(i == 0), stop=(i == NT - 1))
                return last

            def slot_sums_of(e):
                slot_sums(bank[7 if e else 6][:, 2 * e:2 * e + 2], onehot[:, e],
                          lambda i: value[:, i, e, :]).then_inc(slot_psum, 1)

            for e in range(DVE_HOTS):
                pe.wait_ge(onehot_ready, e + 1)
                slot_sums_of(e)

            def rows_transposed(parity, done):
                for b in range(2):
                    for j in range(4):
                        n = 4 * b + j
                        last = pe.transpose(bank[2 + b][:, j * P:(j + 1) * P], gx[:, parity, n * P:(n + 1) * P], ident)
                    if done:
                        last.then_inc(done, 1)
                return last

            def act_transposed():
                for j in range(NF):
                    last = pe.transpose(bank[4][:, j * P:(j + 1) * P], act[:, j * P:(j + 1) * P], ident)
                return last

            def multiply_chunk(n, c, tiles, high, low):
                pe.wait_ge(hi_ready, n + (c + 1))
                for dst, k, cols, start, _ in tiles:
                    pe.matmul(dst, high[:, k, :], w_hi[:, c, cols], start=start, stop=False)
                    pe.matmul(dst, low[:, k, :], w_hi[:, c, cols], start=False, stop=False)
                pe.wait_ge(lo_ready, n + (c + 1))
                for dst, k, cols, _, stop in tiles:
                    last = pe.matmul(dst, high[:, k, :], w_lo[:, c, cols], start=False, stop=stop)
                last.then_inc(used, 1)

            def up_or_gate(m, n, e=None):
                for c in range(CHUNKS):
                    if e is not None and c % 2 == 0:
                        pe.wait_ge(x_hi_ready, e * 2 + (c // 2 + 1))
                        pe.wait_ge(x_lo_ready, e * 2 + (c // 2 + 1))
                    multiply_chunk(n, c, [(bank[m][:, :], 2 * c + a, slice(a * F, (a + 1) * F),
                                           c + a == 0, (c, a) == (CHUNKS - 1, 1)) for a in range(2)], x_hi, x_lo)

            def down(n, first_bank=5):
                for c in range(CHUNKS):
                    multiply_chunk(n, c, [(bank[first_bank + b][:, :], c, slice(b * HALF, (b + 1) * HALF),
                                           c == 0, c == CHUNKS - 1) for b in range(2)], act_hi, act_lo)

            def step(e, s, loads, first=False, more_slots=()):
                n = 0 if first else chunks_before(e)
                up_or_gate(GATE, n, e)
                up_or_gate(UP, n + CHUNKS)
                pe.wait_ge(gx_loaded[1 - s], loads)
                rows_transposed(1 - s, xT_psum)
                for k in more_slots:
                    pe.wait_ge(pool_onehot_ready, k - DVE_HOTS + 1)
                    slot_sums_of(k)
                if not first:
                    pe.wait_ge(act_hi_ready, e)
                    pe.wait_ge(act_lo_ready, e)
                    down(n + 2 * CHUNKS)
                pe.wait_ge(act_ready, e + 1)
                act_transposed().then_inc(actT_psum, 1)

            pe.wait_ge(gx_loaded[0], 16)
            rows_transposed(0, xT_psum)
            pe.wait_ge(weighted_ready, 1)
            for i in range(NT):
                last = pe.transpose(bank[4][:, i * P:(i + 1) * P], weighted[:, i, :], ident)
            last.then_inc(weighted_psum, 1)
            step(0, 0, 16, first=True, more_slots=range(DVE_HOTS, STEP0_HOTS))
            step(1, 1, 32, more_slots=range(STEP0_HOTS, E))
            with pe.Fori(1, E // 2 - 1) as it:
                step(it * 2, 0, it * 16 + 16)
                step(it * 2 + 1, 1, it * 16 + 32)
            step(E - 2, 0, 8 * E)
            n = chunks_before(E - 1)
            up_or_gate(GATE, n, E - 1)
            pe.wait_ge(act_hi_ready, E - 1)
            pe.wait_ge(act_lo_ready, E - 1)
            down(n + CHUNKS, SPARE_BANK)
            up_or_gate(UP, n + 2 * CHUNKS)
            pe.wait_ge(act_ready, E)
            act_transposed().then_inc(actT_psum, 1)
            pe.wait_ge(act_hi_ready, E)
            pe.wait_ge(act_lo_ready, E)
            down(chunks_before(E))
            pe.wait_ge(y_ready, 2 * (E - 1))

            pe.wait_ge(over_ready, 1)
            n_over = pe.value_load(over[0:1, 0:1], min_val=0, max_val=T)
            with pe.If(n_over > 0):
                pe.wait_ge(o_plan, 1)
                for j in range(OV):
                    pe.wait_ge(o_dve, 3 * j + 1)
                    slot_sums(bank[7][:, 0:2], onehot[:, 0], lambda i: ovalue[:, i, j, :]).then_inc(o_pe, 1)
                    pe.wait_ge(o_gx_loaded, 16 * j + 16)
                    rows_transposed(0, None).then_inc(o_pe, 1)
                    pe.wait_ge(o_dve, 3 * j + 2)
                    pe.wait_ge(o_w_loaded, 48 * j + 48)
                    for m in (GATE, UP):
                        for k in range(ND):
                            last = pe.matmul(bank[m][:, :], oxT[:, k, :], raw_at(0, m)[:, k, :],
                                             start=(k == 0), stop=(k == ND - 1))
                    last.then_inc(o_pe, 1)
                    pe.wait_ge(o_dve, 3 * j + 3)
                    act_transposed().then_inc(o_pe, 1)
                    pe.wait_ge(o_act, 4 * j + 2)
                    for b in range(2):
                        for k in range(NF):
                            last = pe.matmul(bank[5 + b][:, :], oactT[:, k, :],
                                             raw_at(0, DOWN)[:, k, b * HALF:(b + 1) * HALF],
                                             start=(k == 0), stop=(k == NF - 1))
                    last.then_inc(o_pe, 1)
            pe.nop()

            pe.wait_ge(weighted_T_ready, 1)
            pe.wait_ge(second_weights_ready, 1)

            def second_parts(i):
                pe.wait_ge(part_loaded[i], 16)
                for b in range(2):
                    pe.matmul(bank[2 * i + b][:, :], second_weights[:, i, :], part[:, i, 1, b * HALF:(b + 1) * HALF],
                              start=True, stop=False)

            def last_results(i):
                for b in range(2):
                    last = pe.matmul(bank[2 * i + b][:, :], weighted_T[:, i, :],
                                     yrow[:, 1, b * HALF:(b + 1) * HALF], start=(i < DVE_PARTS), stop=True)
                last.then_inc(last_psum, 1)

            pe.wait_ge(y_ready, 2 * E)
            for i in range(NT):
                if i >= DVE_PARTS:
                    second_parts(i)
                last_results(i)


def kernel(**inputs):
    import concourse.bacc as bacc
    from concourse.bass_utils import run_bass_kernel_spmd

    def of(name):
        a = np.ascontiguousarray(inputs[name])
        return a if name == "final_norm" else a.reshape(a.shape[1:])

    x = of("x")
    T, D = x.shape
    w_group, w_expert = of("w_group_router"), of("w_expert_router")
    G, E = w_group.shape[1], w_expert.shape[1]
    router = np.concatenate(
        [of("mix_norm").reshape(-1, P).T, of("ffn_norm").reshape(-1, P).T,
         np.broadcast_to(np.concatenate([of("b_group_router"), of("b_expert_router")]), (P, G + E)),
         np.concatenate([w_group, w_expert], 1).reshape(D // P, P, G + E).transpose(1, 0, 2).reshape(P, -1)], 1)
    bands, consts = shape_constants(E, T)
    arrays = {
        "x": x,
        "x_t": np.ascontiguousarray(x.reshape(T // P, P, D // P, P).transpose(3, 0, 2, 1)),
        "router": np.ascontiguousarray(router),
        **{name: of(name) for name in ("pool_w", "pool_scale", "ffn_norm", "w_gate", "w_up", "w_down", "final_norm")},
        "bands": bands,
        "consts": consts,
    }
    nc = bacc.Bacc("TRN2", target_bir_lowering=False, num_devices=1)
    maps, aps = {}, []
    for name, a in arrays.items():
        maps[f"in_{name}"] = a
        aps.append(nc.dram_tensor(f"in_{name}", a.shape, mybir.dt.from_np(a.dtype), kind="ExternalInput").ap())
    aps.append(nc.dram_tensor("out", x.shape, F32, kind="ExternalOutput").ap())
    build(nc, *aps, G)
    r = run_bass_kernel_spmd(nc, [maps], core_ids=[0])
    return r.results[0]["out"].reshape(inputs["x"].shape)
```
